# Optimizing a Trainium2 kernel written in Bass

```python
import math
import jax, jax.numpy as jnp
from jax import lax
import numpy as np

D_MODEL = 1024
BATCH = 1
SEQ = 512
DEPTH = 1

CHUNK = 64
D_MIX = D_MODEL
GDN_HEADS = 4
GDN_HEAD_DIM = 128
GDN_WIDTH = GDN_HEADS * GDN_HEAD_DIM
SC_WIDTH = D_MIX - GDN_WIDTH
SC_GROUPS = 8
GDN_CONV = 4
SC_CONV = 3
D_FF = -(-8 * D_MODEL // (3 * 256)) * 256
RMS_EPS = 1e-6
L2_EPS = 1e-6

Q_OFF = 0
K_OFF = GDN_WIDTH
V_OFF = 2 * GDN_WIDTH
Z_OFF = 3 * GDN_WIDTH
A_OFF = 4 * GDN_WIDTH
BETA_OFF = A_OFF + GDN_HEADS
SCB_OFF = BETA_OFF + GDN_HEADS
SCC_OFF = SCB_OFF + SC_WIDTH
SCH_OFF = SCC_OFF + SC_WIDTH
D_IN = SCH_OFF + SC_WIDTH


def rms_norm(x, w):
    x32 = x.astype(jnp.float32)
    y = x32 * lax.rsqrt(jnp.mean(x32 * x32, axis=-1, keepdims=True) + RMS_EPS)
    return (y * w.astype(jnp.float32)).astype(x.dtype)

def l2_normalize(x):
    x32 = x.astype(jnp.float32)
    return x32 * lax.rsqrt(jnp.sum(x32 * x32, axis=-1, keepdims=True) + L2_EPS)

def causal_depthwise_conv(x, w):
    k_width = w.shape[0]
    s = x.shape[1]
    xp = jnp.pad(x, ((0, 0), (k_width - 1, 0), (0, 0)))
    out = xp[:, 0:s] * w[0]
    for j in range(1, k_width):
        out = out + xp[:, j:j + s] * w[j]
    return out

def gated_delta_rule_chunked(q, k, v, g, beta):
    bsz, s, h, dk = q.shape
    dv = v.shape[-1]
    n = s // CHUNK
    f32 = jnp.float32

    def to_chunks(t):
        return t.astype(f32).reshape(bsz, n, CHUNK, h, -1).transpose(0, 3, 1, 2, 4)

    q = to_chunks(q) * (dk ** -0.5)
    k = to_chunks(k)
    v = to_chunks(v)
    g = g.astype(f32).reshape(bsz, n, CHUNK, h).transpose(0, 3, 1, 2)
    beta = beta.astype(f32).reshape(bsz, n, CHUNK, h).transpose(0, 3, 1, 2)
    g = jnp.cumsum(g, axis=-1)

    k_beta = k * beta[..., None]
    v_beta = v * beta[..., None]
    tril = jnp.tril(jnp.ones((CHUNK, CHUNK), dtype=bool))
    strict = jnp.tril(jnp.ones((CHUNK, CHUNK), dtype=bool), -1)
    decay = jnp.exp(jnp.where(tril, g[..., :, None] - g[..., None, :], -jnp.inf))

    lmat = jnp.where(strict, jnp.einsum('bhncd,bhnmd->bhncm', k_beta, k) * decay, 0.0)
    eye = jnp.broadcast_to(jnp.eye(CHUNK, dtype=f32), lmat.shape)
    tmat = lax.linalg.triangular_solve(lmat, eye, left_side=True, lower=True, unit_diagonal=True)

    u = jnp.einsum('bhncm,bhnme->bhnce', tmat, v_beta)
    w = jnp.einsum('bhncm,bhnmd->bhncd', tmat, k_beta * jnp.exp(g)[..., None])
    attn = jnp.where(tril, jnp.einsum('bhncd,bhnmd->bhncm', q, k) * decay, 0.0)
    g_last = g[..., -1]
    k_dec = k * jnp.exp(g_last[..., None] - g)[..., None]
    q_dec = q * jnp.exp(g)[..., None]

    def step(state, inp):
        qd, wi, ui, ai, kd, gl = inp
        v_new = ui - jnp.einsum('bhcd,bhde->bhce', wi, state)
        out = jnp.einsum('bhcd,bhde->bhce', qd, state) + jnp.einsum('bhcm,bhme->bhce', ai, v_new)
        state = state * jnp.exp(gl)[..., None, None] + jnp.einsum('bhcd,bhce->bhde', kd, v_new)
        return state, out

    xs = tuple(jnp.moveaxis(t, 2, 0) for t in (q_dec, w, u, attn, k_dec, g_last))
    state0 = jnp.zeros((bsz, h, dk, dv), dtype=f32)
    _, outs = lax.scan(step, state0, xs)
    return outs.transpose(1, 0, 3, 2, 4).reshape(bsz, s, h, dv)

def hybrid_mixer(h, w_in, conv_qkv_w, a_log, dt_bias, gdn_norm_w, conv_short_w, w_out):
    bsz, s, _ = h.shape
    p = h @ w_in
    qkv = jax.nn.silu(causal_depthwise_conv(p[..., Q_OFF:Z_OFF], conv_qkv_w))
    q = qkv[..., 0:GDN_WIDTH].reshape(bsz, s, GDN_HEADS, GDN_HEAD_DIM)
    k = qkv[..., GDN_WIDTH:2 * GDN_WIDTH].reshape(bsz, s, GDN_HEADS, GDN_HEAD_DIM)
    v = qkv[..., 2 * GDN_WIDTH:3 * GDN_WIDTH].reshape(bsz, s, GDN_HEADS, GDN_HEAD_DIM)
    z = p[..., Z_OFF:A_OFF].reshape(bsz, s, GDN_HEADS, GDN_HEAD_DIM)
    a = p[..., A_OFF:BETA_OFF].astype(jnp.float32)
    b = p[..., BETA_OFF:SCB_OFF].astype(jnp.float32)
    g = -jnp.exp(a_log.astype(jnp.float32)) * jax.nn.softplus(a + dt_bias.astype(jnp.float32))
    beta = jax.nn.sigmoid(b)
    o = gated_delta_rule_chunked(l2_normalize(q), l2_normalize(k), v, g, beta)
    o = rms_norm(o, gdn_norm_w) * jax.nn.silu(z.astype(jnp.float32))
    y_gdn = o.reshape(bsz, s, GDN_WIDTH).astype(h.dtype)
    sc_b = p[..., SCB_OFF:SCC_OFF]
    sc_c = p[..., SCC_OFF:SCH_OFF]
    sc_h = p[..., SCH_OFF:D_IN]
    y_sc = sc_b * causal_depthwise_conv(sc_c * sc_h, conv_short_w)
    return jnp.concatenate([y_gdn, y_sc], axis=-1) @ w_out

def swiglu(h, w_gate, w_up, w_down):
    return (jax.nn.silu(h @ w_gate) * (h @ w_up)) @ w_down

def first_inputs(seed: int = 0) -> dict:
    key = jax.random.key(seed)
    ks = jax.random.split(key, 20)
    f32 = jnp.float32
    nrm = lambda k, shape, scale: jax.random.normal(k, shape, f32) * scale
    dt = jnp.exp(jax.random.uniform(ks[8], (DEPTH, GDN_HEADS), f32, math.log(1e-3), math.log(1e-1)))
    return {
        "x": nrm(ks[0], (BATCH, SEQ, D_MODEL), 1.0),
        "c": nrm(ks[1], (BATCH, D_MODEL), 1.0),
        "w_ada": nrm(ks[2], (DEPTH, D_MODEL, 6 * D_MODEL), 0.5 * D_MODEL ** -0.5),
        "b_ada": nrm(ks[3], (DEPTH, 6 * D_MODEL), 0.02),
        "norm1_w": 1.0 + nrm(ks[4], (DEPTH, D_MODEL), 0.02),
        "w_in": nrm(ks[5], (DEPTH, D_MODEL, D_IN), D_MODEL ** -0.5),
        "conv_qkv_w": nrm(ks[6], (DEPTH, GDN_CONV, 3 * GDN_WIDTH), GDN_CONV ** -0.5),
        "A_log": jnp.log(jax.random.uniform(ks[7], (DEPTH, GDN_HEADS), f32, 1.0, 16.0)),
        "dt_bias": dt + jnp.log(-jnp.expm1(-dt)),
        "gdn_norm_w": 1.0 + nrm(ks[9], (DEPTH, GDN_HEAD_DIM), 0.02),
        "conv_short_w": nrm(ks[10], (DEPTH, SC_CONV, SC_WIDTH), SC_CONV ** -0.5),
        "w_out": nrm(ks[11], (DEPTH, D_MIX, D_MODEL), D_MIX ** -0.5),
        "norm2_w": 1.0 + nrm(ks[12], (DEPTH, D_MODEL), 0.02),
        "w_gate": nrm(ks[13], (DEPTH, D_MODEL, D_FF), D_MODEL ** -0.5),
        "w_up": nrm(ks[14], (DEPTH, D_MODEL, D_FF), D_MODEL ** -0.5),
        "w_down": nrm(ks[15], (DEPTH, D_FF, D_MODEL), D_FF ** -0.5),
        "norm_f_w": 1.0 + nrm(ks[16], (D_MODEL,), 0.02),
    }

def first_block(x, c, w_ada, b_ada, norm1_w, w_in, conv_qkv_w, A_log, dt_bias, gdn_norm_w,
              conv_short_w, w_out, norm2_w, w_gate, w_up, w_down, norm_f_w):
    c_act = jax.nn.silu(c)
    for l in range(DEPTH):
        mod = (c_act @ w_ada[l] + b_ada[l])[:, None, :]
        shift1, scale1, gate1, shift2, scale2, gate2 = jnp.split(mod, 6, axis=-1)
        h = rms_norm(x, norm1_w[l]) * (1.0 + scale1) + shift1
        x = x + gate1 * hybrid_mixer(h, w_in[l], conv_qkv_w[l], A_log[l], dt_bias[l],
                                     gdn_norm_w[l], conv_short_w[l], w_out[l])
        h = rms_norm(x, norm2_w[l]) * (1.0 + scale2) + shift2
        x = x + gate2 * swiglu(h, w_gate[l], w_up[l], w_down[l])
    return rms_norm(x, norm_f_w)


SSM_D_INNER = D_MODEL
SSM_HEAD_DIM = 64
SSM_HEADS = SSM_D_INNER // SSM_HEAD_DIM
SSM_GROUPS = 4
SSM_STATE = 128
SSM_CONV = 4
SSM_CHUNK = 128
SSM_CONV_DIM = SSM_D_INNER + 2 * SSM_GROUPS * SSM_STATE
ATT_D = D_MODEL
ATT_HEAD_DIM = 64
ATT_HEADS = ATT_D // ATT_HEAD_DIM
ATT_BLOCK = 128
IN_SPLITS = (SSM_D_INNER, SSM_CONV_DIM, SSM_HEADS, ATT_D, ATT_D, ATT_D, ATT_HEADS, ATT_D, D_MODEL, D_MODEL)
IN_COLS = SSM_D_INNER + SSM_CONV_DIM + SSM_HEADS + 4 * ATT_D + ATT_HEADS + 2 * D_MODEL


def _offsets(sizes):
    out, acc = [], 0
    for s in sizes[:-1]:
        acc += s
        out.append(acc)
    return out

def _rmsnorm(x, g):
    xf = x.astype(jnp.float32)
    y = xf * lax.rsqrt(jnp.mean(xf * xf, axis=-1, keepdims=True) + RMS_EPS) * g.astype(jnp.float32)
    return y.astype(x.dtype)

def _causal_dwconv(u, w, b):
    y = lax.conv_general_dilated(u, w[:, None, :].astype(u.dtype), window_strides=(1,),
                                 padding=((SSM_CONV - 1, 0),),
                                 dimension_numbers=('NWC', 'WIO', 'NWC'),
                                 feature_group_count=u.shape[-1])
    return y + b.astype(u.dtype)

def _ssd_chunked(xs, dt, a, b_mat, c_mat, d_skip):
    bsz, seqlen, n_heads, p = xs.shape
    g, n = b_mat.shape[2], b_mat.shape[3]
    r = n_heads // g
    nc = seqlen // SSM_CHUNK
    q = SSM_CHUNK
    xdt = (xs * dt[..., None]).reshape(bsz, nc, q, g, r, p)
    bc = b_mat.reshape(bsz, nc, q, g, n)
    cc = c_mat.reshape(bsz, nc, q, g, n)
    da_cs = jnp.cumsum((dt * a).reshape(bsz, nc, q, g, r), axis=2)
    causal = jnp.tril(jnp.ones((q, q), dtype=bool))
    seg = da_cs[:, :, :, None] - da_cs[:, :, None, :]
    decay = jnp.exp(jnp.where(causal[None, None, :, :, None, None], seg, -jnp.inf))
    cb = jnp.einsum('bclgn,bcsgn->bclsg', cc, bc)
    y_diag = jnp.einsum('bclsgr,bcsgrp->bclgrp', cb[..., None] * decay, xdt)
    to_end = jnp.exp(da_cs[:, :, -1:] - da_cs)
    states = jnp.einsum('bcsgn,bcsgrp->bcgrpn', bc, xdt * to_end[..., None])
    chunk_decay = jnp.exp(da_cs[:, :, -1])

    def step(carry, inp):
        st, dec = inp
        return carry * dec[..., None, None] + st, carry

    init = jnp.zeros((bsz, g, r, p, n), states.dtype)
    _, prev = lax.scan(step, init, (jnp.moveaxis(states, 1, 0), jnp.moveaxis(chunk_decay, 1, 0)))
    prev = jnp.moveaxis(prev, 0, 1)
    y_off = jnp.einsum('bclgn,bcgrpn->bclgrp', cc, prev) * jnp.exp(da_cs)[..., None]
    y = (y_diag + y_off).reshape(bsz, seqlen, n_heads, p)
    return y + xs * d_skip[:, None]

def _forgetting_attention(q, k, v, log_f):
    seqlen = q.shape[2]
    scale = ATT_HEAD_DIM ** -0.5
    fcum = jnp.cumsum(log_f, axis=-1)
    outs = []
    for blk in range(seqlen // ATT_BLOCK):
        q0, q1 = blk * ATT_BLOCK, (blk + 1) * ATT_BLOCK
        s = jnp.einsum('bhqd,bhkd->bhqk', q[:, :, q0:q1], k[:, :, :q1]).astype(jnp.float32) * scale
        s = s + fcum[:, :, q0:q1, None] - fcum[:, :, None, :q1]
        qpos = q0 + jnp.arange(ATT_BLOCK)
        kpos = jnp.arange(q1)
        s = jnp.where(kpos[None, :] <= qpos[:, None], s, -jnp.inf)
        prob = jax.nn.softmax(s, axis=-1)
        outs.append(jnp.einsum('bhqk,bhkd->bhqd', prob.astype(v.dtype), v[:, :, :q1]))
    return jnp.concatenate(outs, axis=2)

def _hybrid_layer(x, pre_g, w_in, conv_w, conv_b, dt_bias, a_log, d_skip, ssm_norm_g,
                  fgate_b, w_branch_ssm, w_branch_att, w_out, post_g):
    bsz, seqlen, _ = x.shape
    f32 = jnp.float32
    h = _rmsnorm(x, pre_g)
    proj = jnp.einsum('bld,de->ble', h, w_in)
    z_ssm, xbc, dt_raw, q, k, v, f_raw, z_att, g_ssm, g_att = jnp.split(proj, _offsets(IN_SPLITS), axis=-1)

    xbc = jax.nn.silu(_causal_dwconv(xbc, conv_w, conv_b))
    gn = SSM_GROUPS * SSM_STATE
    xs, b_ssm, c_ssm = jnp.split(xbc, [SSM_D_INNER, SSM_D_INNER + gn], axis=-1)
    dt = jax.nn.softplus(dt_raw.astype(f32) + dt_bias.astype(f32))
    a = -jnp.exp(a_log.astype(f32))
    y = _ssd_chunked(xs.astype(f32).reshape(bsz, seqlen, SSM_HEADS, SSM_HEAD_DIM), dt, a,
                     b_ssm.astype(f32).reshape(bsz, seqlen, SSM_GROUPS, SSM_STATE),
                     c_ssm.astype(f32).reshape(bsz, seqlen, SSM_GROUPS, SSM_STATE),
                     d_skip.astype(f32))
    yg = (y.reshape(bsz, seqlen, SSM_D_INNER) * jax.nn.silu(z_ssm.astype(f32)))
    yg = yg.reshape(bsz, seqlen, SSM_GROUPS, SSM_D_INNER // SSM_GROUPS)
    yg = yg * lax.rsqrt(jnp.mean(yg * yg, axis=-1, keepdims=True) + RMS_EPS)
    y_ssm = (yg.reshape(bsz, seqlen, SSM_D_INNER) * ssm_norm_g.astype(f32)).astype(x.dtype)

    def heads(t):
        return t.reshape(bsz, seqlen, ATT_HEADS, ATT_HEAD_DIM).transpose(0, 2, 1, 3)
    log_f = jax.nn.log_sigmoid(f_raw.astype(f32) + fgate_b.astype(f32)).transpose(0, 2, 1)
    o = _forgetting_attention(heads(q), heads(k), heads(v), log_f)
    o = o.transpose(0, 2, 1, 3).reshape(bsz, seqlen, ATT_D)
    y_att = (o.astype(f32) * jax.nn.silu(z_att.astype(f32))).astype(x.dtype)

    p_ssm = jnp.einsum('ble,ed->bld', y_ssm, w_branch_ssm)
    p_att = jnp.einsum('ble,ed->bld', y_att, w_branch_att)
    merged = jax.nn.sigmoid(g_ssm) * p_ssm + jax.nn.sigmoid(g_att) * p_att
    out = jnp.einsum('bld,de->ble', merged, w_out)
    return x + _rmsnorm(out, post_g)

def second_inputs(seed: int = 0) -> dict:
    key = jax.random.key(seed)
    ks = jax.random.split(key, 16)
    f32 = jnp.float32
    nl = DEPTH
    nrm = jax.random.normal
    x = nrm(ks[0], (BATCH, SEQ, D_MODEL), f32)
    pre_norm_g = 1.0 + 0.05 * nrm(ks[1], (nl, D_MODEL), f32)
    w_in = nrm(ks[2], (nl, D_MODEL, IN_COLS), f32) * D_MODEL ** -0.5
    conv_w = nrm(ks[3], (nl, SSM_CONV, SSM_CONV_DIM), f32) * SSM_CONV ** -0.5
    conv_b = 0.02 * nrm(ks[4], (nl, SSM_CONV_DIM), f32)
    dt0 = jnp.exp(jax.random.uniform(ks[5], (nl, SSM_HEADS), f32, minval=math.log(1e-3), maxval=math.log(1e-1)))
    dt_bias = dt0 + jnp.log(-jnp.expm1(-dt0))
    a_log = jnp.log(jax.random.uniform(ks[6], (nl, SSM_HEADS), f32, minval=1.0, maxval=16.0))
    d_skip = 1.0 + 0.1 * nrm(ks[7], (nl, SSM_HEADS), f32)
    ssm_norm_g = 1.0 + 0.05 * nrm(ks[8], (nl, SSM_D_INNER), f32)
    fgate_b = jax.random.uniform(ks[9], (nl, ATT_HEADS), f32, minval=1.0, maxval=4.0)
    w_branch_ssm = nrm(ks[10], (nl, SSM_D_INNER, D_MODEL), f32) * SSM_D_INNER ** -0.5
    w_branch_att = nrm(ks[11], (nl, ATT_D, D_MODEL), f32) * ATT_D ** -0.5
    w_out = nrm(ks[12], (nl, D_MODEL, D_MODEL), f32) * D_MODEL ** -0.5
    post_norm_g = 1.0 + 0.05 * nrm(ks[13], (nl, D_MODEL), f32)
    return {'x': x, 'pre_norm_g': pre_norm_g, 'w_in': w_in, 'conv_w': conv_w, 'conv_b': conv_b,
            'dt_bias': dt_bias, 'a_log': a_log, 'd_skip': d_skip, 'ssm_norm_g': ssm_norm_g,
            'fgate_b': fgate_b, 'w_branch_ssm': w_branch_ssm, 'w_branch_att': w_branch_att,
            'w_out': w_out, 'post_norm_g': post_norm_g}

def second_block(x, pre_norm_g, w_in, conv_w, conv_b, dt_bias, a_log, d_skip, ssm_norm_g,
              fgate_b, w_branch_ssm, w_branch_att, w_out, post_norm_g):
    for i in range(DEPTH):
        x = _hybrid_layer(x, pre_norm_g[i], w_in[i], conv_w[i], conv_b[i], dt_bias[i], a_log[i],
                          d_skip[i], ssm_norm_g[i], fgate_b[i], w_branch_ssm[i], w_branch_att[i],
                          w_out[i], post_norm_g[i])
    return x


def setup_inputs(seed=0):
    out = dict(first_inputs(seed))
    for name, value in second_inputs(seed + 1).items():
        if name != "x":
            out[name + "_2"] = value
    return out


def reference(
    x, c, w_ada, b_ada, norm1_w, w_in, conv_qkv_w, A_log, dt_bias, gdn_norm_w, conv_short_w,
    w_out, norm2_w, w_gate, w_up, w_down, norm_f_w, pre_norm_g_2, w_in_2, conv_w_2, conv_b_2,
    dt_bias_2, a_log_2, d_skip_2, ssm_norm_g_2, fgate_b_2, w_branch_ssm_2, w_branch_att_2,
    w_out_2, post_norm_g_2,
):
    x = first_block(
        x, c, w_ada, b_ada, norm1_w, w_in, conv_qkv_w, A_log, dt_bias, gdn_norm_w, conv_short_w,
        w_out, norm2_w, w_gate, w_up, w_down, norm_f_w,
    )
    return second_block(
        x, pre_norm_g_2, w_in_2, conv_w_2, conv_b_2, dt_bias_2, a_log_2, d_skip_2, ssm_norm_g_2,
        fgate_b_2, w_branch_ssm_2, w_branch_att_2, w_out_2, post_norm_g_2,
    )


_drawn_inputs = setup_inputs


def setup_inputs(seed=0):
    import zlib

    import numpy as np

    out = dict(_drawn_inputs(seed))
    spreads = {}
    factors = {'norm1_w': 4.298, 'gdn_norm_w': 48.699, 'norm2_w': 35.129, 'conv_b_2': 2.716}
    for name, (base, spread) in spreads.items():
        noise = np.random.default_rng([zlib.crc32(name.encode()), seed]).standard_normal(out[name].shape)
        drawn = base * np.exp(spread * noise) if base else spread * noise
        out[name] = __import__('jax').numpy.asarray(drawn.astype(out[name].dtype))
    for name, factor in factors.items():
        out[name] = (out[name] * factor).astype(out[name].dtype)
    return out
```

```python
import concourse.bass as bass
from concourse import mybir

F32 = mybir.dt.float32
F32R = mybir.dt.float32r
ALU = mybir.AluOpType
ACT = mybir.ActivationFunctionType
AX = mybir.AxisListType
ds = bass.ds

P = 128
T = 512
NT = T // P
D = 1024
KD = D // P
DFF = 2816
KF = DFF // P
KH = KF // 2
HG = 4
HS = 16
G = 4
HPG = HS // G
NEG = -1.0e30
L2_EPS = 1e-6
RMS_EPS = 1e-6

Q1, K1, V1, Z1, AB1 = 0, 512, 1024, 1536, 2048
SCB1, SCC1, SCH1 = 2056, 2568, 3080
Z2, XBC2, DT2, Q2, K2, V2, F2, ZA2, GS2, GA2 = 0, 1024, 3072, 3088, 4112, 5136, 6160, 6176, 7200, 8224

BADA, CVEC, N1, N2, NF, PRE, POST, SSMG, CB, GN = 0, 48, 56, 64, 72, 80, 88, 96, 104, 120
CQKV, CSC, CX = 0, 48, 60

CSROW, NFROW = 16, 32
SHIFT1, SCALE1, GATE1, SHIFT2, SCALE2, GATE2 = 0, 8, 16, 24, 32, 40


class Count:

    def __init__(self, nc, name):
        self.name, self.sem = name, nc.alloc_semaphore(name)
        self.n, self.per, self.reg = 0, 0, None

    def mark(self, ins, by=1):
        ins.then_inc(self.sem, by)
        self.n += by
        return (self, self.n)

    def now(self):
        return (self, self.n)


class Engine:

    def __init__(self, nc, eng, name):
        self.eng, self.count, self.seen = eng, Count(nc, name), {}

    def wait(self, *tickets):
        for t in tickets:
            if t is None:
                continue
            c, n = t
            if self.seen.get(c.name, 0) >= n:
                continue
            self.seen[c.name] = n
            self.eng.wait_ge(c.sem, n + c.reg * c.per if c.per else n)

    def do(self, fn, *args, after=(), **kw):
        self.wait(*after)
        return self.count.mark(fn(*args, **kw))

    def now(self):
        return self.count.now()


class Machine:
    def __init__(self, nc, learned):
        self.nc, self.learned = nc, learned
        self.pe = Engine(nc, nc.tensor, "pe")
        self.act = Engine(nc, nc.scalar, "act")
        self.dve = Engine(nc, nc.vector, "dve")
        self.pool = Engine(nc, nc.gpsimd, "pool")
        self.sp = Engine(nc, nc.sync, "sp")
        self.tiles = Count(nc, "tiles_done")
        self.loaded = [Count(nc, f"raw_loaded{s}") for s in range(RAW)]
        self.released = [Count(nc, f"raw_released{s}") for s in range(RAW)]
        self.hi_done = [Count(nc, f"hi_done{s}") for s in range(2)]
        self.extra = []
        self.held = {}

    def counts(self):
        return [e.count for e in (self.pe, self.act, self.dve, self.pool, self.sp)] + [self.tiles] + \
            self.loaded + self.released + self.hi_done + self.extra

    def count(self, name):
        c = Count(self.nc, name)
        self.extra.append(c)
        return c

    def compute(self):
        return (self.pe, self.act, self.dve, self.pool)

    def all_now(self):
        return [c.now() for c in self.extra if c.name == "scratch_written" and c.n] + [self.pe.now(), self.act.now(), self.dve.now(), self.pool.now(), self.tiles.now()]

    def fence(self):
        now = self.all_now()
        for e in self.compute():
            e.wait(*now)

    def loop(self, name, turns, body):
        base = {c.name: c.n for c in self.counts()}
        before = dict(self.held)
        if name not in self.learned:
            body(0)
            per = {c.name: c.n - base[c.name] for c in self.counts()}
            ends = {k: (t[0].name, t[1] - base[t[0].name]) for k, t in self.held.items() if before.get(k) != t}
            for c in self.counts():
                c.n = base[c.name] + per[c.name] * turns
            self.learned[name] = (per, ends)
            for e in (*self.compute(), self.sp):
                e.seen = {}
            return
        per, ends = self.learned[name]
        by_name = {c.name: c for c in self.counts()}
        for k, (cname, off) in ends.items():
            c, pre = by_name[cname], before.get(k)
            carried = base[cname] + off - per[cname]
            if pre is not None and not (pre[0] is c and pre[1] <= carried):
                for e in self.compute():
                    e.wait(pre)
            self.held[k] = (c, carried) if carried > 0 else None
        with self.nc.Fori(0, turns) as i:
            for c in self.counts():
                c.per, c.reg = per[c.name], i
            for e in (*self.compute(), self.sp):
                e.seen = {}
            body(i)
        for c in self.counts():
            assert c.n - base[c.name] == per[c.name], (name, c.name)
            c.n, c.per, c.reg = base[c.name] + per[c.name] * turns, 0, None
        for e in (*self.compute(), self.sp):
            e.seen = {}
        for k, (cname, off) in ends.items():
            self.held[k] = (by_name[cname], base[cname] + off + per[cname] * (turns - 1))


RAW = 4
SLOT = KH * P


class Memory:

    def __init__(self, nc, base, end):
        self.nc, self.at, self.end, self.n = nc, base, end, 0

    def take(self, name, shape, dtype=F32):
        size = 4
        for s in shape[1:]:
            size *= s
        off, self.at = self.at, self.at + (size + 31) // 32 * 32
        assert self.at <= self.end, (name, self.at, self.end)
        return self.nc.alloc_sbuf_tensor_at(name, shape, dtype, offset=off)


def program(nc, learned, stop, x, c, w_ada, b_ada, norm1_w, w_in, conv_qkv_w, A_log, dt_bias, gdn_norm_w,
            conv_short_w, w_out, norm2_w, w_gate, w_up, w_down, norm_f_w, pre_norm_g_2, w_in_2,
            conv_w_2, conv_b_2, dt_bias_2, a_log_2, d_skip_2, ssm_norm_g_2, fgate_b_2,
            w_branch_ssm_2, w_branch_att_2, w_out_2, post_norm_g_2, out):
    m = Machine(nc, learned)
    pe, act, dve, pool, sp = m.pe, m.act, m.dve, m.pool, m.sp
    held = m.held
    base = (nc.sbuf_base + 31) // 32 * 32
    mem = Memory(nc, base, nc.sbuf_usable_end)

    xT = mem.take("xT", [P, KD, T])
    fin_at = mem.at
    a_hi = mem.take("a_hi", [P, KD, T], F32R)
    a_lo = mem.take("a_lo", [P, KD, T], F32R)
    raw = [mem.take(f"raw{s}", [P, SLOT]) for s in range(RAW)]
    w_hi = [mem.take(f"w_hi{s}", [P, SLOT], F32R) for s in range(2)]
    w_lo = [mem.take(f"w_lo{s}", [P, SLOT], F32R) for s in range(2)]
    ident = mem.take("ident", [P, P])
    ones = mem.take("ones", [P, P])
    causal = mem.take("causal", [P, P])
    strict = mem.take("strict", [P, P])
    negmask = mem.take("negmask", [P, P])
    LEVELS = 7
    level = [mem.take(f"level{s}", [P, P]) for s in range(LEVELS)]
    col_a = mem.take("col_a", [P, P])
    col_b = mem.take("col_b", [P, P])
    col_d = mem.take("col_d", [P, KD])
    mod = mem.take("mod", [P, 48])
    cact = mem.take("cact", [P, KD])
    gain1 = mem.take("gain1", [P, KD])
    gain2 = mem.take("gain2", [P, KD])
    eps = mem.take("eps", [P, 1])
    gcols = mem.take("gcols", [P, NT, 8])
    bcols = mem.take("bcols", [P, NT, 8])
    dtcols = mem.take("dtcols", [P, NT, HS])
    cscols = mem.take("cscols", [P, NT, HS])
    norm_col = mem.take("norm_col", [P, 3 * NT])
    rowc = mem.take("rowc", [P, 8])
    work = mem.at
    half = Memory(nc, work, nc.sbuf_usable_end)
    hid_hi = half.take("hid_hi", [P, KF, T], F32R)
    hid_lo = half.take("hid_lo", [P, KF, T], F32R)
    mlp = half
    mem_b = Memory(nc, work, nc.sbuf_usable_end)
    b_hi = mem_b.take("b_hi", [P, KD, T], F32R)
    b_lo = mem_b.take("b_lo", [P, KD, T], F32R)
    work = mem_b.at

    bank = [nc.alloc_psum_tensor(f"bank{i}", [P, T], F32) for i in range(8)]

    def v3(t, a=NT):
        return t.rearrange("p (a n) -> p a n", a=a)

    def across(t, n=NT):
        return t.unsqueeze(1).broadcast_to([P, n, P])

    def along(t, n=P):
        return t.unsqueeze(2).broadcast_to([P, t.shape[1], n])

    pair_in = m.count("pair_in")
    x_in = m.count("x_in")

    def load(tiles):
        nc.disable_value_cache = True
        for j, t in enumerate(tiles):
            s = j % RAW
            sp.wait((m.released[s], m.loaded[s].n // 16) if m.loaded[s].n else None)
            dst = raw[s][:, 0:t["nk"] * t["n"]].rearrange("p (k n) -> p k n", n=t["n"])
            with nc.allow_non_contiguous_dma(reason="the few columns of the decay projections"):
                if t.get("pairs") is not None:
                    nc.sync.dma_start(dst[:, :, 0:32], t["pairs"][0]).then_inc(pair_in.sem, 16)
                    dst, src = dst[:, :, 32:64], t["pairs"][1]
                else:
                    src = t["src"].rearrange("(k p) n -> p k n", p=P)
                m.loaded[s].mark(nc.sync.dma_start(dst, src), 16)
        nc.disable_value_cache = False

    def split(s, q, size):
        need = 16 * (m.released[s].n + 1)
        act.wait((m.loaded[s], need), m.tiles.now())
        hi = m.hi_done[q].mark(nc.scalar.activation(w_hi[q][:, 0:size], raw[s][:, 0:size], ACT.Copy))
        dve.wait(hi, m.tiles.now())
        held[f"pair{q}"] = m.released[s].mark(nc.vector.tensor_tensor(
            w_lo[q][:, 0:size], raw[s][:, 0:size], w_hi[q][:, 0:size].bitcast(F32), ALU.subtract))

    def dense(tiles, nxt, k_after=None):
        load(tiles)
        splits = [j for j, t in enumerate(tiles) if not t.get("plain")]
        for j, t in enumerate(tiles):
            s, o, n = j % RAW, t["out"], t["n"]
            bk = t["bank"]
            if t.get("plain"):
                pe.wait((m.loaded[s], 16 * (m.released[s].n + 1)), held.get(f"bank{bk}"))
                for k in range(t["nk"]):
                    ins = nc.tensor.matmul(o, raw[s][:, k * n:(k + 1) * n], t["x"](k), start=(k == 0),
                                           stop=(k == t["nk"] - 1))
                done = m.released[s].mark(ins)
                if t.get("evac"):
                    t["evac"](done)
                yield
                continue
            at = splits.index(j)
            q = at % 2
            late = False
            if at + 1 < len(splits):
                j2 = splits[at + 1]
                split(j2 % RAW, (at + 1) % 2, tiles[j2]["nk"] * tiles[j2]["n"])
            elif nxt:
                late = (at + 1) % 2 == 1
                if not late:
                    split(0, 0, nxt)
            pe.wait(held[f"pair{q}"] if late or True else None, held.get(f"bank{bk}"))
            for k in range(t["nk"]):
                hi_k, lo_k = w_hi[q][:, k * n:(k + 1) * n], w_lo[q][:, k * n:(k + 1) * n]
                x_hi, x_lo = t["x"](k)
                if k_after and j == 0:
                    pe.wait(k_after[k])
                first, last = k == 0 and t.get("start", True), k == t["nk"] - 1 and t.get("stop", True)
                nc.tensor.matmul(o, hi_k, x_hi, start=first, stop=False)
                nc.tensor.matmul(o, hi_k, x_lo, start=False, stop=False)
                ins = nc.tensor.matmul(o, lo_k, x_hi, start=False, stop=last)
                if k < t["nk"] - 1:
                    yield
            done = m.tiles.mark(ins)
            if late:
                split(0, 0, nxt)
            if t.get("evac"):
                t["evac"](done)
            yield

    def run(gen):
        for _ in gen:
            pass

    def weave(mixer, products, ratio):
        due = 0.0
        for _ in mixer:
            due += ratio
            while due >= 1:
                next(products, None)
                due -= 1
        run(products)

    def a_in(k):
        return a_hi[:, k, :], a_lo[:, k, :]

    def b_in(k):
        return b_hi[:, k, :], b_lo[:, k, :]

    def wtile(src, xs, bk, evac, nk=KD, n=P, **kw):
        return dict(src=src, nk=nk, n=n, x=xs, bank=bk, out=bank[bk][0:n, :], evac=evac, **kw)

    def to_hi_lo(value, hi, lo, after):
        t_hi = act.do(nc.scalar.activation, hi, value, ACT.Copy, after=after)
        return dve.do(nc.vector.tensor_tensor, lo, value, hi.bitcast(F32), ALU.subtract, after=[t_hi, *after])

    def conv(src, acc, taps, after):
        t = dve.do(nc.vector.tensor_scalar, acc[:, :], src[:, :], taps[-1], None, ALU.mult, after=after)
        for s in range(1, len(taps)):
            t = dve.do(nc.vector.scalar_tensor_tensor, acc[:, s:T], src[:, 0:T - s], taps[-1 - s], acc[:, s:T],
                       ALU.mult, ALU.add, after=[t])
        return t

    t0 = pool.do(nc.gpsimd.memset, ident[:], 0.0)
    ones_t = pool.do(nc.gpsimd.memset, ones[:], 1.0)
    eps_t = pool.do(nc.gpsimd.memset, eps[:], RMS_EPS)
    norm_c = pool.do(nc.gpsimd.memset, norm_col[:, 2 * NT:3 * NT], -0.5)
    tn = pool.do(nc.gpsimd.memset, negmask[:], 0.0)
    ident_t = pool.do(nc.gpsimd.affine_select, out=ident[:], in_=ident[:], compare_op=ALU.not_equal, fill=1.0,
                      base=0, pattern=[[-1, P]], channel_multiplier=1, after=[tn])
    pool.do(nc.gpsimd.affine_select, out=causal[:], in_=ones[:], compare_op=ALU.is_ge, fill=0.0,
            base=0, pattern=[[1, P]], channel_multiplier=-1)
    pool.do(nc.gpsimd.affine_select, out=strict[:], in_=ones[:], compare_op=ALU.is_ge, fill=0.0,
            base=-1, pattern=[[1, P]], channel_multiplier=-1)
    masks_t = pool.do(nc.gpsimd.affine_select, out=negmask[:], in_=negmask[:], compare_op=ALU.is_ge, fill=NEG,
                      base=0, pattern=[[-1, P]], channel_multiplier=1)
    for s in range(LEVELS):
        h = 1 << s
        nb = P // (2 * h)
        v = level[s][:].rearrange("p (b e) -> p b e", b=nb)
        t = pool.do(nc.gpsimd.memset, level[s][:], 0.0)
        t = pool.do(nc.gpsimd.memset, v[:, :, h:2 * h], 1.0, after=[t])
        t = pool.do(nc.gpsimd.affine_select, out=v, in_=v, compare_op=ALU.is_ge, fill=0.0, base=0,
                    pattern=[[-2 * h, nb], [0, 2 * h]], channel_multiplier=1, after=[t])
        masks_t = pool.do(nc.gpsimd.affine_select, out=v, in_=v, compare_op=ALU.is_ge, fill=0.0, base=h - 1,
                          pattern=[[2 * h, nb], [0, 2 * h]], channel_multiplier=-1, after=[t])

    setup = Memory(nc, work, nc.sbuf_usable_end)
    xt = setup.take("x_tokens", [P, NT, D])
    pack_a = setup.take("pack_a", [P, P])
    pack_b = setup.take("pack_b", [P, P])
    pack_d = setup.take("pack_d", [P, P])
    skip2 = setup.take("skip2", [KD, 2])
    su_sq = [setup.take(f"su_sq{i}", [P, T]) for i in range(2)]
    su_acc = setup.take("su_acc", [P, T])
    su_rstd = setup.take("su_rstd", [P, T])
    su_h = [setup.take(f"su_h{i}", [P, T]) for i in range(2)]
    vec_in = m.count("vec_in")

    def rows(v):
        return v.rearrange("a (t p) -> (a t) p", p=P) if len(v.shape) == 2 else v.rearrange("(t p) -> t p", p=P)

    zero_rows = pool.do(nc.gpsimd.memset, rowc[:], 0.0)
    for pack, at, v in ((pack_a, CVEC, c), (pack_a, BADA, b_ada), (pack_a, N1, norm1_w), (pack_a, N2, norm2_w),
                        (pack_a, NF, norm_f_w), (pack_a, PRE, pre_norm_g_2), (pack_a, POST, post_norm_g_2),
                        (pack_a, SSMG, ssm_norm_g_2), (pack_a, CB, conv_b_2), (pack_a, GN, gdn_norm_w),
                        (pack_b, CQKV, conv_qkv_w[0]), (pack_b, CSC, conv_short_w[0]), (pack_b, CX, conv_w_2[0])):
        r = rows(v)
        vec_in.mark(nc.scalar.dma_start(pack[at:at + r.shape[0], :], r), 16)
    for t in range(NT):
        x_in.mark(nc.gpsimd.dma_start(xt[:, t, :], x[0, t * P:(t + 1) * P, :]), 16)
    with nc.allow_non_contiguous_dma(reason="a few dozen numbers, one per head"):
        vec_in.mark(nc.scalar.dma_start(skip2[:], d_skip_2[0].rearrange("(t h) -> t h", h=2)), 16)
        act.wait(zero_rows)
        for col, at, v in ((0, 0, dt_bias[0]), (1, 0, A_log[0]), (2, 0, dt_bias_2[0]), (3, 0, a_log_2[0]),
                           (4, 32, fgate_b_2[0])):
            vec_in.mark(nc.scalar.dma_start(rowc[at:at + v.shape[0], col:col + 1], v.unsqueeze(1)), 16)
    vec_t = vec_in.now()

    skip_t = dve.do(nc.vector.tensor_copy, pack_d[0:KD, :].rearrange("t (h p) -> t h p", h=2),
                    skip2[:].unsqueeze(2).broadcast_to([KD, 2, P // 2]), after=[vec_t])
    pe.wait(ident_t, vec_t, skip_t)
    for b_, pack, n, col in ((0, pack_a, GN + 1, col_a), (1, pack_b, CX + 64, col_b), (2, pack_d, KD, col_d)):
        t = pe.do(nc.tensor.transpose, bank[b_][:, 0:n], pack[0:n, :], ident[0:n, 0:n])
        cols_t = dve.do(nc.vector.tensor_copy, col[:, 0:n], bank[b_][:, 0:n], after=[t])
        held[f"bank{b_}"] = cols_t
    cact_t = act.do(nc.scalar.activation, cact[:], col_a[:, CVEC:CVEC + KD], ACT.Silu, after=[cols_t])

    def squares(k, src, sq, acc, after):
        if k == 0:
            return act.do(nc.scalar.activation, acc, src, ACT.Square, after=[held.get("acc"), *after])
        t = act.do(nc.scalar.activation, sq[k % 2], src, ACT.Square, after=[held.get(f"sq{k % 2}"), *after])
        t = dve.do(nc.vector.tensor_tensor, acc, acc, sq[k % 2], ALU.add, after=[t, held["sum"]])
        held[f"sq{k % 2}"] = t
        return t

    pe.wait(*[(x_in, 64)])
    for k in range(KD):
        b_ = 3 + k % 4
        pe.wait(held.get(f"bank{b_}"))
        for t in range(NT):
            ins = nc.tensor.transpose(bank[b_][:, t * P:(t + 1) * P], xt[:, t, k * P:(k + 1) * P], ident[:])
        t = pe.count.mark(ins)
        t = dve.do(nc.vector.tensor_copy, xT[:, k, :], bank[b_][:], after=[t])
        held[f"bank{b_}"] = t
        held["sum"] = squares(k, xT[:, k, :], [su_sq[0][:], su_sq[1][:]], su_acc[:], [t])

    def inv_rms(acc, rstd, bk, n, after, eps_=RMS_EPS):
        pe.wait(held.get(f"bank{bk}"), *after)
        for t in range(NT):
            ins = nc.tensor.matmul(bank[bk][:, t:t + 1], acc[:, t * P:(t + 1) * P], ones[:, 0:1], start=True, stop=True)
        t = pe.count.mark(ins)
        c0 = norm_col[:, 0:NT]
        t = dve.do(nc.vector.tensor_scalar, c0, bank[bk][:, 0:NT], 1.0 / n, eps_, ALU.mult, ALU.add, after=[t])
        t = pool.do(nc.gpsimd.tensor_tensor, norm_col[:, NT:2 * NT], c0, norm_col[:, 2 * NT:3 * NT], ALU.pow,
                    after=[t, norm_c])
        pe.wait(t)
        for k in range(NT):
            ins = nc.tensor.matmul(bank[bk][:, k * P:(k + 1) * P], norm_col[:, NT + k:NT + k + 1].broadcast_to([P, P]),
                                   ident[:], start=True, stop=True)
        t = pe.count.mark(ins)
        t = act.do(nc.scalar.activation, rstd[:], bank[bk][:], ACT.Copy, after=[t])
        held[f"bank{bk}"] = t
        return t

    def apply_norm(src, rstd, gain, shift, tmp, after):
        out_t = []
        for k in range(KD):
            h = tmp[k % 2]
            t = dve.do(nc.vector.scalar_tensor_tensor, h, src[:, k, :], gain[:, k:k + 1], rstd[:], ALU.mult, ALU.mult,
                       after=[held.get(f"tmp{k % 2}"), *after])
            if shift is None:
                t = to_hi_lo(h, a_hi[:, k, :], a_lo[:, k, :], [t])
            else:
                hi = act.do(nc.scalar.activation, a_hi[:, k, :], h, ACT.Identity, bias=shift[:, k:k + 1], after=[t])
                t = dve.do(nc.vector.scalar_tensor_tensor, a_lo[:, k, :], h, shift[:, k:k + 1],
                           a_hi[:, k, :].bitcast(F32), ALU.add, ALU.subtract, after=[hi])
            held[f"tmp{k % 2}"] = t
            out_t.append(t)
        return out_t

    def ada_tile(t0, j, bk, evac=None):
        t = dict(src=w_ada[0][:, ds(t0 * P + j * P, P)], nk=KD, n=P, plain=True,
                 x=lambda k: cact[:, k:k + 1], bank=bk, out=bank[bk][:, j:j + 1], evac=evac)
        return t

    def ada_evac(t0, n, bk):
        def go(done):
            held[f"bank{bk}"] = held["mod"] = dve.do(
                nc.vector.tensor_tensor, mod[:, ds(t0, n)], bank[bk][:, 0:n], col_a[:, ds(BADA + t0, n)], ALU.add,
                after=[done])
        return go

    pe.wait(cact_t)
    run(dense([ada_tile(0, j, 7, ada_evac(0, 16, 7) if j == 15 else None) for j in range(16)], 0))
    mod_t = held["mod"]
    t = dve.do(nc.vector.scalar_tensor_tensor, gain1[:], mod[:, SCALE1:SCALE1 + KD], 1.0, col_a[:, N1:N1 + KD],
               ALU.add, ALU.mult, after=[mod_t])
    pe.wait(ones_t)
    act.wait(eps_t)
    rt = inv_rms(su_acc[:], su_rstd, 2, D, [held["sum"]])
    h_t = apply_norm(xT, su_rstd, gain1, mod[:, SHIFT1:SHIFT1 + KD], [su_h[0][:], su_h[1][:]], [t, rt])

    scratch = nc.dram_tensor("row_scratch", [3 * HS, T], F32).ap()
    scratch_w = m.count("scratch_written")
    gsm = Memory(nc, setup.at, nc.sbuf_usable_end)
    r_s = [gsm.take(f"r_s{i}", [64, T]) for i in range(3)]
    reset = gsm.take("reset", [64, T])
    r_a, r_b, r_c = (r[:, :] for r in r_s)

    def softplus(x_, y, u, r_, nrow, p0, after):
        X, Y, U = x_[p0:p0 + nrow, :], y[p0:p0 + nrow, :], u[p0:p0 + nrow, :]
        t = act.do(nc.scalar.activation, Y, X, ACT.Abs, after=after)
        t = act.do(nc.scalar.activation, Y, Y, ACT.Exp, scale=-1.0, after=[t])
        t = dve.do(nc.vector.tensor_scalar, U, Y, 1.0, None, ALU.add, after=[t])
        t = dve.do(nc.vector.scalar_tensor_tensor, Y, U, -1.0, Y, ALU.add, ALU.subtract, after=[t])
        R = r_[p0:p0 + nrow, :]
        t1 = dve.do(nc.vector.reciprocal, R, U, after=[t])
        t = dve.do(nc.vector.scalar_tensor_tensor, Y, Y, -1.0, R, ALU.mult, ALU.mult, after=[t1])
        t2 = act.do(nc.scalar.activation, U, U, ACT.Ln, after=[t])
        t = dve.do(nc.vector.tensor_tensor, Y, Y, U, ALU.add, after=[t2])
        return dve.do(nc.vector.scalar_tensor_tensor, Y, X, 0.0, Y, ALU.max, ALU.add, after=[t])

    def chunk_reset(nrow):
        t = pool.do(nc.gpsimd.memset, reset[0:nrow, :], 1.0)
        return pool.do(nc.gpsimd.memset, v3(reset[0:nrow, :])[:, :, 0:1], 0.0, after=[t])

    reset_t = chunk_reset(64)
    t = act.do(nc.scalar.activation, rowc[0:HS, 5:6], rowc[0:HS, 1:2], ACT.Exp, after=[vec_t])
    t = act.do(nc.scalar.activation, rowc[0:HS, 6:7], rowc[0:HS, 3:4], ACT.Exp, after=[t])
    na_t = dve.do(nc.vector.tensor_scalar, rowc[0:HS, 5:7], rowc[0:HS, 5:7], -1.0, None, ALU.mult, after=[t])

    def ab_evac(done):
        src = bank[0][0:8, :]
        t = dve.do(nc.vector.tensor_scalar, r_a[0:8, :], src, rowc[0:8, 0:1], None, ALU.add, after=[done, na_t])
        t2 = act.do(nc.scalar.activation, gsb[0:8, :], src, ACT.Exp, scale=-1.0, after=[t])
        held["bank0"] = t2
        t2 = dve.do(nc.vector.tensor_scalar, gsb[0:8, :], gsb[0:8, :], 1.0, None, ALU.add, after=[t2])
        beta_t = dve.do(nc.vector.reciprocal, gsb[0:8, :], gsb[0:8, :], after=[t2])
        t = softplus(r_a, r_b, gsu, r_c, 8, 0, [t, t2])
        t = dve.do(nc.vector.tensor_scalar, r_b[0:8, :], r_b[0:8, :], rowc[0:8, 5:6], None, ALU.mult, after=[t])
        t = dve.do(nc.vector.tensor_tensor_scan, gsg[0:8, :], reset[0:8, :], r_b[0:8, :], 0.0, ALU.mult, ALU.add,
                   after=[t, reset_t])
        act.wait(t, beta_t)
        scratch_w.mark(nc.scalar.dma_start(scratch[0:4, :], gsg[0:4, :]), 16)
        scratch_w.mark(nc.scalar.dma_start(scratch[4:8, :], gsb[4:8, :]), 16)
        pe.wait(t, beta_t, held.get("bank2"))
        for i, s_ in enumerate((gsg, gsb)):
            for j in range(NT):
                ins = nc.tensor.transpose(bank[2][:, i * 64 + j * 8:i * 64 + j * 8 + 8], s_[0:8, j * P:(j + 1) * P],
                                          ident[0:8, 0:8])
        t = pe.count.mark(ins)
        dve.do(nc.vector.tensor_copy, gcols[:], bank[2][:, 0:32].rearrange("p (a n) -> p a n", a=NT), after=[t])
        held["bank2"] = held["gb"] = dve.do(nc.vector.tensor_copy, bcols[:],
                                            bank[2][:, 64:96].rearrange("p (a n) -> p a n", a=NT))

    gsb = gsm.take("gsb", [64, T])
    gsu = gsm.take("gsu", [64, T])
    gsg = gsm.take("gsg", [64, T])
    win1 = w_in[0]
    ab = wtile(win1[:, AB1:AB1 + 8], a_in, 0, ab_evac, n=8)
    split_ab = dict(ab)
    def first_split(tiles):
        load(tiles)
        split(0, 0, tiles[0]["nk"] * tiles[0]["n"])

    def dense_first(tiles, nxt, k_after=None):
        act_need = 16 * (m.released[0].n + 1)
        g = dense(tiles, nxt, k_after)
        split(0, 0, tiles[0]["nk"] * tiles[0]["n"])
        run(g)

    dense_first([ab], KD * P, h_t)

    gw = Memory(nc, work, nc.sbuf_usable_end)
    F = lambda name, shape=(P, T): gw.take(name, list(shape))
    st_q, st_k, st_v, st_z = (F(f"st_{n}") for n in "qkvz")
    qT, kT, vT, sz = (F(f"g_{n}") for n in ("qT", "kT", "vT", "sz"))
    kb, kbe, qd = F("kb"), F("kbe"), F("qd")
    gB, bB, eg = F("gB"), F("bB"), F("eg")
    DTi, DTs = F("DTi"), F("DTs")
    LTt, ATt = F("LT"), F("AT")
    Ms = [F(f"M{s}") for s in range(LEVELS)]
    Xf, XT, Yc = F("X"), F("XT"), F("Yc")
    kdec, vb = F("kdec"), F("vb")
    Rs, vn = F("Rs", (P, P)), F("vn", (P, P))
    Sst = [F(f"S{i}", (P, P)) for i in range(2)]
    sqA = F("sqA")
    cS, uS = F("cS"), F("uS")
    hconv = F("hconv", (P, 3, 4))
    sconv = F("sconv", (P, 3))
    hcol = F("hcol", (P, 16))
    m.fence()

    def gdn_products(i, last=False):
        off = ds(i * P, P) if not isinstance(i, int) else slice(i * P, (i + 1) * P)

        def cols(base_):
            return win1[:, ds(base_ + i * P, P)]
        one = ds(i, 1)
        hc = dve.do(nc.vector.tensor_copy, hconv[:].unsqueeze(3),
                    col_b[:, CQKV:CQKV + 48].rearrange("p (j s h) -> p s j h", j=4, s=3)[:, :, :, one])
        hc2 = dve.do(nc.vector.tensor_copy, sconv[:].unsqueeze(2),
                     col_b[:, CSC:CSC + 12].rearrange("p (j t) -> p j t", j=3)[:, :, one])

        def conv_evac(part, dst, bk):
            def go(done):
                held[f"bank{bk}"] = held[f"st{part}"] = conv(
                    bank[bk], dst, [hconv[:, part, j:j + 1] for j in range(4)], [done, hc, held.get(f"used{part}")])
            return go

        def z_evac(done):
            held["bank1"] = held["st3"] = act.do(nc.scalar.activation, st_z[:], bank[1][:], ACT.Copy,
                                                 after=[done, held.get("used3")])

        def c_evac(done):
            held["bank0"] = held["cS"] = act.do(nc.scalar.activation, cS[:], bank[0][:], ACT.Copy,
                                                after=[done, held.get("cS_used")])

        def h_evac(done):
            t = dve.do(nc.vector.tensor_tensor, uS[:], cS[:], bank[1][:], ALU.mult, after=[done, held["cS"]])
            held["bank1"] = t
            held["u"] = conv(uS, cS, [sconv[:, j:j + 1] for j in range(3)], [t, hc2])

        def b_evac(done):
            t = dve.do(nc.vector.tensor_tensor, uS[:], cS[:], bank[0][:], ALU.mult, after=[done, held["u"]])
            held["bank0"] = t
            hi = b_hi[:, ds(i + HG, 1), :].rearrange("p a n -> p (a n)")
            lo = b_lo[:, ds(i + HG, 1), :].rearrange("p a n -> p (a n)")
            held["cS_used"] = to_hi_lo(uS[:], hi, lo, [t])

        tiles = [wtile(cols(Q1), a_in, 0, conv_evac(0, st_q, 0)),
                 wtile(cols(K1), a_in, 1, conv_evac(1, st_k, 1)),
                 wtile(cols(V1), a_in, 0, conv_evac(2, st_v, 0)),
                 wtile(cols(Z1), a_in, 1, z_evac),
                 wtile(cols(SCC1), a_in, 0, c_evac),
                 wtile(cols(SCH1), a_in, 1, h_evac),
                 wtile(cols(SCB1), a_in, 0, b_evac)]
        t0 = GATE1 + i * 8
        mixed = []
        for j, t in enumerate(tiles):
            mixed += [t, ada_tile(t0, j, 7)]
        mixed[-1:] = [ada_tile(t0, 6, 7), ada_tile(t0, 7, 7, ada_evac(t0, 8, 7))]
        return dense(mixed, KD * P)

    rows_in = m.count("rows_in")
    Y_, Z_, ZT_, O_, S_ = 2, 3, 4, 5, 6

    def gdn_mix(i):
        before = m.all_now()
        for e in (act, dve, pool):
            e.wait(*before)
        act.wait(scratch_w.now())
        rows_in.mark(nc.scalar.dma_start(gB[:], scratch[ds(i, 1), :].partition_broadcast(P).rearrange("p a n -> p (a n)")), 16)
        rows_in.mark(nc.scalar.dma_start(bB[:], scratch[ds(i + 4, 1), :].partition_broadcast(P).rearrange("p a n -> p (a n)")), 16)
        rows_t = rows_in.now()
        t = dve.do(nc.vector.tensor_copy, hcol[:, 0:NT].unsqueeze(2), gcols[:, :, ds(i, 1)])
        hc_t = dve.do(nc.vector.tensor_copy, hcol[:, NT:2 * NT].unsqueeze(2), bcols[:, :, ds(i + 4, 1)])
        st = [held[f"st{j}"] for j in range(4)]
        tq, tk, tv, tz = (act.do(nc.scalar.activation, dst[:], src[:], ACT.Silu, after=[s_])
                          for dst, src, s_ in ((qT, st_q, st[0]), (kT, st_k, st[1]), (vT, st_v, st[2]), (sz, st_z, st[3])))
        for j, t in enumerate((tq, tk, tv, tz)):
            held[f"used{j}"] = t
        t1 = act.do(nc.scalar.activation, sqA[:], qT[:], ACT.Square, after=[tq])
        t2 = act.do(nc.scalar.activation, Yc[:], kT[:], ACT.Square, after=[tk])
        yield
        pe.wait(*before)
        t1 = inv_rms(sqA[:], sqA, Y_, 1, [t1], L2_EPS)
        t2 = inv_rms(Yc[:], Yc, Z_, 1, [t2], L2_EPS)
        tq = dve.do(nc.vector.scalar_tensor_tensor, qT[:], qT[:], float(P) ** -0.5, sqA[:], ALU.mult, ALU.mult, after=[t1])
        tk = dve.do(nc.vector.tensor_tensor, kT[:], kT[:], Yc[:], ALU.mult, after=[t2])
        for t in range(NT):
            dt_ = dve.do(nc.vector.tensor_scalar, DTi[:, t * P:(t + 1) * P], gB[:, t * P:(t + 1) * P],
                         hcol[:, t:t + 1], 0.0, ALU.subtract, ALU.min, after=[rows_t, hc_t])
        te = act.do(nc.scalar.activation, eg[:], gB[:], ACT.Exp, after=[rows_t])
        t = act.do(nc.scalar.activation, DTi[:], DTi[:], ACT.Exp, after=[dt_])
        tkb = dve.do(nc.vector.tensor_tensor, kb[:], kT[:], bB[:], ALU.mult, after=[tk])
        tdi = dve.do(nc.vector.tensor_tensor, v3(DTs[:]), v3(DTi[:]), across(strict[:]), ALU.mult, after=[t])
        tda = dve.do(nc.vector.tensor_tensor, v3(DTi[:]), v3(DTi[:]), across(causal[:]), ALU.mult, after=[tdi])
        yield
        pe.wait(tkb)
        for t in range(NT):
            cc = slice(t * P, (t + 1) * P)
            ins = nc.tensor.matmul(bank[Y_][:, cc], kT[:, cc], kb[:, cc], start=True, stop=True)
        tY = pe.count.mark(ins)
        tL = dve.do(nc.vector.tensor_tensor, LTt[:], bank[Y_][:], DTs[:], ALU.mult, after=[tY, tdi])
        yield
        tM = []
        for s in range(LEVELS):
            tM.append(pool.do(nc.gpsimd.tensor_tensor, v3(Ms[s][:]), v3(LTt[:]), across(level[s][:]), ALU.mult,
                              after=[tL, masks_t]))
        pe.wait(tq)
        for t in range(NT):
            cc = slice(t * P, (t + 1) * P)
            ins = nc.tensor.matmul(bank[Z_][:, cc], kT[:, cc], qT[:, cc], start=True, stop=True)
        tZ = pe.count.mark(ins)
        tA = dve.do(nc.vector.tensor_tensor, ATt[:], bank[Z_][:], DTi[:], ALU.mult, after=[tZ, tda])
        tkbe = dve.do(nc.vector.tensor_tensor, kbe[:], kb[:], eg[:], ALU.mult, after=[te])
        tqd = dve.do(nc.vector.tensor_tensor, qd[:], qT[:], eg[:], ALU.mult)
        yield
        pe.wait(tv)
        for t in range(NT):
            cc = slice(t * P, (t + 1) * P)
            ins = nc.tensor.transpose(bank[ZT_][:, cc], kT[:, cc], ident[:])
        tkt = pe.count.mark(ins)
        for t in range(NT):
            cc = slice(t * P, (t + 1) * P)
            ins = nc.tensor.transpose(bank[O_][:, cc], vT[:, cc], ident[:])
        tvt = pe.count.mark(ins)
        glast = v3(gB[:])[:, :, P - 1:P]
        t = dve.do(nc.vector.tensor_tensor, hcol[:, 8:12].unsqueeze(2), glast, hcol[:, 0:NT].unsqueeze(2), ALU.subtract)
        t = act.do(nc.scalar.activation, hcol[:, 8:12], hcol[:, 8:12], ACT.Exp, after=[t])
        tkd = dve.do(nc.vector.tensor_tensor, v3(kdec[:]), v3(bank[ZT_][:]), along(hcol[:, 8:12]), ALU.mult, after=[tkt, t])
        tvb = dve.do(nc.vector.tensor_tensor, v3(vb[:]), v3(bank[O_][:]), along(hcol[:, 4:8]), ALU.mult, after=[tvt])
        yield
        pe.wait(tM[0])
        for t in range(NT):
            cc = slice(t * P, (t + 1) * P)
            ins = nc.tensor.transpose(bank[Y_][:, cc], Ms[0][:, cc], ident[:])
        tY = pe.count.mark(ins)
        tXT = dve.do(nc.vector.tensor_tensor, v3(XT[:]), across(ident[:]), v3(Ms[0][:]), ALU.subtract, after=[tM[0]])
        tX = dve.do(nc.vector.tensor_tensor, v3(Xf[:]), across(ident[:]), v3(bank[Y_][:]), ALU.subtract, after=[tY])
        yield
        for s in range(1, LEVELS):
            pe.wait(tX, tM[s])
            for t in range(NT):
                cc = slice(t * P, (t + 1) * P)
                ins = nc.tensor.matmul(bank[Y_][:, cc], Ms[s][:, cc], Xf[:, cc], start=True, stop=True)
            t = pe.count.mark(ins)
            tYc = act.do(nc.scalar.activation, Yc[:], bank[Y_][:], ACT.Copy, after=[t])
            yield
            pe.wait(tYc, tXT)
            for t in range(NT):
                cc = slice(t * P, (t + 1) * P)
                ins = nc.tensor.matmul(bank[ZT_][:, cc], Yc[:, cc], XT[:, cc], start=True, stop=True)
            tZT = pe.count.mark(ins)
            if s < LEVELS - 1:
                for t in range(NT):
                    cc = slice(t * P, (t + 1) * P)
                    ins = nc.tensor.matmul(bank[Z_][:, cc], XT[:, cc], Yc[:, cc], start=True, stop=True)
                tZ = pe.count.mark(ins)
                tX = dve.do(nc.vector.tensor_tensor, Xf[:], Xf[:], bank[Z_][:], ALU.subtract, after=[tZ])
            tXT = dve.do(nc.vector.tensor_tensor, XT[:], XT[:], bank[ZT_][:], ALU.subtract, after=[tZT, tX])
            yield
        tS, tvn, tO = None, None, None
        pe.wait(tXT, tkbe, tqd, tA, tkd, tvb)
        for t in range(NT):
            cc = slice(t * P, (t + 1) * P)
            S_in, S_out = Sst[(t + 1) % 2], Sst[t % 2]
            if t == 0:
                rhs = vb[:, cc]
            else:
                t1 = pe.do(nc.tensor.matmul, bank[S_][:, 0:P], kbe[:, cc], S_in[:], start=True, stop=True, after=[tS])
                t1 = dve.do(nc.vector.tensor_tensor, Rs[:], vb[:, cc], bank[S_][:, 0:P], ALU.subtract, after=[t1])
                rhs = Rs[:]
                pe.do(nc.tensor.matmul, bank[O_][:, cc], S_in[:], qd[:, cc], start=True, stop=False)
                pe.wait(t1)
                yield
            t1 = pe.do(nc.tensor.matmul, bank[S_][:, P:2 * P], XT[:, cc], rhs, start=True, stop=True)
            tvn = act.do(nc.scalar.activation, vn[:], bank[S_][:, P:2 * P], ACT.Copy, after=[t1])
            yield
            if t < NT - 1:
                t1 = pe.do(nc.tensor.matmul, bank[S_][:, 2 * P:3 * P], kdec[:, cc], vn[:], start=True, stop=True, after=[tvn])
                if t == 0:
                    tS = dve.do(nc.vector.tensor_copy, S_out[:], bank[S_][:, 2 * P:3 * P], after=[t1])
                else:
                    tS = dve.do(nc.vector.scalar_tensor_tensor, S_out[:], S_in[:], eg[:, (t + 1) * P - 1:(t + 1) * P],
                                bank[S_][:, 2 * P:3 * P], ALU.mult, ALU.add, after=[t1])
            tO = pe.do(nc.tensor.matmul, bank[O_][:, cc], vn[:], ATt[:, cc], start=(t == 0), stop=True, after=[tvn])
            yield
        t = act.do(nc.scalar.activation, sqA[:], bank[O_][:], ACT.Square, after=[tO])
        yield
        t = inv_rms(sqA[:], sqA, Y_, P, [t])
        t = dve.do(nc.vector.scalar_tensor_tensor, Yc[:], bank[O_][:], col_a[:, GN:GN + 1], sqA[:], ALU.mult, ALU.mult, after=[t])
        t = dve.do(nc.vector.tensor_tensor, Yc[:], Yc[:], sz[:], ALU.mult, after=[t])
        to_hi_lo(Yc[:], b_hi[:, ds(i, 1), :].rearrange("p a n -> p (a n)"),
                 b_lo[:, ds(i, 1), :].rearrange("p a n -> p (a n)"), [t])
        yield

    run(gdn_products(0))
    m.loop("delta_net", HG - 1, lambda i: weave(gdn_mix(i), gdn_products(i + 1), 2.2))
    run(gdn_mix(HG - 1))
    m.fence()

    p_sq = [gw.take(f"p_sq{i}", [P, T]) for i in range(0)]
    pw = Memory(nc, mlp.at, nc.sbuf_usable_end)
    acc = pw.take("p_acc", [P, T])
    sq2 = [pw.take(f"p_sq{i}", [P, T]) for i in range(2)]
    sgate = pw.take("p_sgate", [P, T])
    hval = pw.take("p_hval", [P, T])
    rstd = pw.take("p_rstd", [P, T])
    tmpn = [sq2[0][:], sgate[:]]

    def residual(mt, bk, gate):
        def go(done):
            xk = xT[:, mt, :]
            t = dve.do(nc.vector.scalar_tensor_tensor, xk, bank[bk][:], gate[:, mt:mt + 1], xk, ALU.mult, ALU.add,
                       after=[done])
            held[f"bank{bk}"] = t
            held["sum"] = squares(mt, xk, [sq2[0][:], sq2[1][:]], acc[:], [t])
        return go

    held["acc"] = held["sq0"] = held["sq1"] = None
    run(dense([wtile(w_out[0][:, mt * P:(mt + 1) * P], b_in, mt % 2, residual(mt, mt % 2, mod[:, GATE1:GATE1 + KD]))
               for mt in range(KD)], KD * P))
    t = dve.do(nc.vector.scalar_tensor_tensor, gain2[:], mod[:, SCALE2:SCALE2 + KD], 1.0, col_a[:, N2:N2 + KD],
               ALU.add, ALU.mult)
    rt = inv_rms(acc[:], rstd, 2, D, [held["sum"]])
    m.fence()
    held["tmp0"] = held["tmp1"] = None
    h_t = apply_norm(xT, rstd, gain2, mod[:, SHIFT2:SHIFT2 + KD], tmpn, [t, rt])

    def hidden(i, nxt, k_after=None):
        tiles = []
        for j in range(2):
            def gate_evac(done, bk=2 * j):
                held[f"bank{bk}"] = held["silu"] = act.do(nc.scalar.activation, sgate[:], bank[bk][:], ACT.Silu,
                                                          after=[done, held.get("silu_used")])

            def up_evac(done, bk=2 * j + 1, j=j):
                t = dve.do(nc.vector.tensor_tensor, hval[:], sgate[:], bank[bk][:], ALU.mult,
                           after=[done, held["silu"], held.get("hval_used")])
                held[f"bank{bk}"] = held["silu_used"] = t
                one = ds(i * 2 + j, 1)
                held["hval_used"] = to_hi_lo(hval[:], hid_hi[:, one, :].rearrange("p a n -> p (a n)"),
                                             hid_lo[:, one, :].rearrange("p a n -> p (a n)"), [t])
            cs = ds(i * 2 * P + j * P, P)
            tiles += [wtile(w_gate[0][:, cs], a_in, 2 * j, gate_evac), wtile(w_up[0][:, cs], a_in, 2 * j + 1, up_evac)]
        return dense(tiles, nxt, k_after)

    pe.wait(*h_t)
    act.wait(*h_t)
    dve.wait(*h_t)
    m.loop("mlp_hidden", KF // 2 - 1, lambda i: run(hidden(i, KD * P)))
    run(hidden(KF // 2 - 1, KH * P))
    m.fence()

    def down(mt, half_):
        lo_row = half_ * KH

        def x_of(k):
            return hid_hi[:, lo_row + k, :], hid_lo[:, lo_row + k, :]
        ev = residual(mt, mt % 2, mod[:, GATE2:GATE2 + KD]) if half_ else None
        return wtile(w_down[0][lo_row * P:(lo_row + KH) * P, mt * P:(mt + 1) * P], x_of, mt % 2, ev, nk=KH,
                     start=(half_ == 0), stop=(half_ == 1))

    held["acc"] = held["sq0"] = held["sq1"] = None
    run(dense([down(mt, h) for mt in range(KD) for h in range(2)], 0))
    rt = inv_rms(acc[:], rstd, 2, D, [held["sum"]])
    m.fence()
    held["acc"] = held["sq0"] = held["sq1"] = None
    for k in range(KD):
        t = dve.do(nc.vector.scalar_tensor_tensor, xT[:, k, :], xT[:, k, :], col_a[:, NF + k:NF + k + 1], rstd[:],
                   ALU.mult, ALU.mult, after=[rt])
        held["sum"] = squares(k, xT[:, k, :], [sq2[0][:], sq2[1][:]], acc[:], [t])

    out_c = m.count("out_stored")

    def store(src, add=None):
        m.fence()
        ow = Memory(nc, work, nc.sbuf_usable_end)
        toks = [ow.take(f"o_tok{t}", [P, D]) for t in range(NT)]
        for t in range(NT):
            for h in range(2):
                b_ = 2 * (t % 2) + h
                pe.wait(held.get(f"bank{b_}"))
                for k in range(4):
                    ins = nc.tensor.transpose(bank[b_][:, k * P:(k + 1) * P], src[:, h * 4 + k, t * P:(t + 1) * P], ident[:])
                tt = pe.count.mark(ins)
                e, fn = (act, None) if h else (dve, None)
                if h:
                    tt = act.do(nc.scalar.activation, toks[t][:, h * T:(h + 1) * T], bank[b_][:], ACT.Copy, after=[tt])
                else:
                    tt = dve.do(nc.vector.tensor_copy, toks[t][:, h * T:(h + 1) * T], bank[b_][:], after=[tt])
                held[f"bank{b_}"] = tt
                sp.wait(tt)
            out_c.mark(nc.sync.dma_start(out[0, t * P:(t + 1) * P, :], toks[t][:]), 16)
        sp.wait(out_c.now())

    if stop == 1:
        return store(xT)

    m.fence()
    held["tmp0"] = held["tmp1"] = None
    rw = Memory(nc, pw.at, nc.sbuf_usable_end)
    r2 = Memory(nc, work, nc.sbuf_usable_end)
    rx, ry, ru, rcs, rcum = (r2.take(f"r2_{n}", [64, T]) for n in ("x", "y", "u", "cs", "cum"))
    rr, reset2 = r2.take("r2_r", [64, T]), r2.take("r2_reset", [64, T])
    rcsum = [r2.take(f"r2_rsq{i}", [P, NT]) for i in range(2)]
    z_t = pool.do(nc.gpsimd.memset, rx[:], 0.0)
    t = pool.do(nc.gpsimd.memset, reset2[:], 1.0)
    reset_t = pool.do(nc.gpsimd.memset, v3(reset2[:, :])[:, :, 0:1], 0.0, after=[t])

    def dtf_evac(done):
        dve.do(nc.vector.tensor_scalar, rx[0:HS, :], bank[0][0:HS, :], rowc[0:HS, 2:3], None, ALU.add, after=[done, z_t])
        t = dve.do(nc.vector.tensor_scalar, rx[32:32 + HS, :], bank[0][32:32 + HS, :], rowc[32:32 + HS, 4:5], -1.0,
                   ALU.add, ALU.mult)
        held["bank0"] = t
        t = softplus(rx, ry, ru, rr, 64, 0, [t])
        t1 = dve.do(nc.vector.tensor_scalar, rcs[0:HS, :], ry[0:HS, :], rowc[0:HS, 6:7], None, ALU.mult, after=[t])
        t1 = dve.do(nc.vector.tensor_tensor_scan, rcum[0:HS, :], reset2[0:HS, :], rcs[0:HS, :], 0.0, ALU.mult, ALU.add,
                    after=[t1, reset_t])
        t2 = pool.do(nc.gpsimd.memset, rcs[32:32 + HS, :], 1.0, after=[pool.now()])
        t2 = dve.do(nc.vector.tensor_tensor_scan, rcum[32:32 + HS, :], rcs[32:32 + HS, :], ry[32:32 + HS, :], 0.0,
                    ALU.mult, ALU.add, after=[t2])
        act.wait(t1, t2)
        scratch_w.mark(nc.scalar.dma_start(scratch[CSROW:CSROW + HS, :], rcum[0:HS, :]), 16)
        scratch_w.mark(nc.scalar.dma_start(scratch[NFROW:NFROW + HS, :], rcum[32:32 + HS, :]), 16)
        pe.wait(t1, held.get("bank2"))
        for i, s_ in enumerate((ry, rcum)):
            for j in range(NT):
                ins = nc.tensor.transpose(bank[2][:, i * 64 + j * HS:i * 64 + j * HS + HS], s_[0:HS, j * P:(j + 1) * P],
                                          ident[0:HS, 0:HS])
        t = pe.count.mark(ins)
        dve.do(nc.vector.tensor_copy, dtcols[:], v3(bank[2][:, 0:64]), after=[t])
        held["bank2"] = dve.do(nc.vector.tensor_copy, cscols[:], v3(bank[2][:, 64:128]))

    win2 = w_in_2[0]
    dtf = wtile(None, a_in, 0, dtf_evac, n=64)
    dtf["pairs"] = [win2[:, c0:c0 + 32].rearrange("(k p) n -> p k n", p=P) for c0 in (DT2, F2)]
    t = inv_rms(acc[:], rstd, 2, D, [held["sum"]])
    h_t = apply_norm(xT, rstd, col_a[:, PRE:PRE + KD], None, tmpn, [t])
    act.wait((pair_in, 16))
    dve.wait((pair_in, 16))
    dense_first([dtf], KD * P, h_t)
    m.fence()

    sw = Memory(nc, work, nc.sbuf_usable_end)
    F = lambda name, shape=(P, T): sw.take("s_" + name, list(shape))
    st2 = [F(f"st{j}") for j in range(6)]
    xs = [F(f"xs{j}") for j in range(2)]
    BT, CT = F("BT"), F("CT")
    szs = [F(f"sz{j}") for j in range(2)]
    csB, Ch = F("csB", (P, HPG, T)), F("Ch", (P, HPG, T))
    cbm, Btok = F("cbm"), F("Btok")
    xdt, xde = F("xdt", (P, NT, 2 * P)), F("xde", (P, NT, 2 * P))
    ST = [F(f"ST{t}", (P, 2 * P)) for t in range(1, NT)]
    yv = [F(f"yv{j}") for j in range(2)]
    ysq = [F(f"ysq{j}") for j in range(2)]
    xconv, xbias = F("xconv", (P, 4, 4)), F("xbias", (P, 8))
    hcs, hdt, tend, dec = (F(n, (P, NT, HPG)) for n in ("hcs", "hdt", "tend", "dec"))

    def ssm_products(g):
        taps = col_b[:, CX:CX + 64].rearrange("p (j t) -> p t j", j=4)
        dve.do(nc.vector.tensor_copy, xconv[:, 0:2, :], taps[:, ds(g * 2, 2), :])
        dve.do(nc.vector.tensor_copy, xconv[:, 2:3, :], taps[:, ds(g + 2 * G, 1), :])
        xc = dve.do(nc.vector.tensor_copy, xconv[:, 3:4, :], taps[:, ds(g + 3 * G, 1), :])

        def conv_evac(j, bk):
            def go(done):
                held[f"bank{bk}"] = held[f"st{j}"] = conv(
                    bank[bk], st2[j], [xconv[:, j, a:a + 1] for a in range(4)], [done, xc, held.get(f"used{j}")])
            return go

        def z_evac(j, bk):
            def go(done):
                held[f"bank{bk}"] = held[f"st{j}"] = act.do(nc.scalar.activation, st2[j][:], bank[bk][:], ACT.Copy,
                                                            after=[done, held.get(f"used{j}")])
            return go

        def cols(base_, per):
            return win2[:, ds(base_ + g * per, P)]
        BC = XBC2 + D
        return dense([wtile(cols(XBC2, 2 * P), a_in, 0, conv_evac(0, 0)),
                      wtile(cols(XBC2 + P, 2 * P), a_in, 1, conv_evac(1, 1)),
                      wtile(cols(BC, P), a_in, 0, conv_evac(2, 0)),
                      wtile(cols(BC + G * P, P), a_in, 1, conv_evac(3, 1)),
                      wtile(cols(Z2, 2 * P), a_in, 0, z_evac(4, 0)),
                      wtile(cols(Z2 + P, 2 * P), a_in, 1, z_evac(5, 1))], KD * P)

    def ssm_mix(g):
        before = m.all_now()
        for e in (act, dve, pool):
            e.wait(*before)
        act.wait(scratch_w.now())
        rows_t = rows_in.mark(nc.scalar.dma_start(
            csB[:], scratch[ds(g * HPG + CSROW, HPG), :].partition_broadcast(P)), 16)
        dve.do(nc.vector.tensor_copy, hcs[:], cscols[:, :, ds(g * HPG, HPG)])
        dve.do(nc.vector.tensor_copy, hdt[:], dtcols[:, :, ds(g * HPG, HPG)])
        dve.do(nc.vector.tensor_copy, xbias[:, 0:2], col_a[:, ds(g * 2 + CB, 2)])
        dve.do(nc.vector.tensor_copy, xbias[:, 2:3], col_a[:, ds(g + CB + 2 * G, 1)])
        dve.do(nc.vector.tensor_copy, xbias[:, 3:4], col_a[:, ds(g + CB + 3 * G, 1)])
        dve.do(nc.vector.tensor_copy, xbias[:, 4:6], col_a[:, ds(g * 2 + SSMG, 2)])
        xb = dve.do(nc.vector.tensor_copy, xbias[:, 6:8], col_d[:, ds(g * 2, 2)])
        tt = []
        for j, dst in enumerate((xs[0], xs[1], BT, CT)):
            tt.append(act.do(nc.scalar.activation, dst[:], st2[j][:], ACT.Silu, bias=xbias[:, j:j + 1],
                             after=[held[f"st{j}"], xb]))
            held[f"used{j}"] = tt[-1]
        for j in range(2):
            tt.append(act.do(nc.scalar.activation, szs[j][:], st2[4 + j][:], ACT.Silu, after=[held[f"st{4 + j}"]]))
            held[f"used{4 + j}"] = tt[-1]
        yield
        pe.wait(*before, tt[3])
        for t in range(NT):
            cc = slice(t * P, (t + 1) * P)
            ins = nc.tensor.matmul(bank[2][:, cc], BT[:, cc], CT[:, cc], start=True, stop=True)
        t = pe.count.mark(ins)
        tcb = dve.do(nc.vector.tensor_tensor, v3(cbm[:]), v3(bank[2][:]), across(causal[:]), ALU.mult, after=[t])
        yield
        for t in range(NT):
            cc = slice(t * P, (t + 1) * P)
            ins = nc.tensor.transpose(bank[3][:, cc], BT[:, cc], ident[:])
        t = pe.count.mark(ins)
        tB = act.do(nc.scalar.activation, Btok[:], bank[3][:], ACT.Copy, after=[t])
        yield
        for u in range(2):
            for t in range(2):
                for j in range(2):
                    cc = slice((2 * u + t) * P, (2 * u + t + 1) * P)
                    ins = nc.tensor.transpose(bank[4 + u][:, t * 2 * P + j * P:t * 2 * P + (j + 1) * P], xs[j][:, cc], ident[:])
            t = pe.count.mark(ins)
            tx = dve.do(nc.vector.tensor_tensor,
                        xdt[:, 2 * u:2 * u + 2, :].rearrange("p t (h c) -> p t h c", h=HPG),
                        bank[4 + u][:].rearrange("p (t h c) -> p t h c", t=2, h=HPG),
                        hdt[:, 2 * u:2 * u + 2, :].unsqueeze(3).broadcast_to([P, 2, HPG, 64]), ALU.mult, after=[t])
            yield
        last = csB[:].rearrange("p h (t n) -> p t h n", t=NT)[:, :, :, P - 1]
        t = dve.do(nc.vector.tensor_tensor, tend[:], last, hcs[:], ALU.subtract, after=[rows_t])
        tend_t = act.do(nc.scalar.activation, tend[:], tend[:], ACT.Exp, after=[t])
        dec_t = act.do(nc.scalar.activation, dec[:], last, ACT.Exp)
        txe = dve.do(nc.vector.tensor_tensor, xde[:].rearrange("p t (h c) -> p t h c", h=HPG),
                     xdt[:].rearrange("p t (h c) -> p t h c", h=HPG),
                     tend[:].unsqueeze(3).broadcast_to([P, NT, HPG, 64]), ALU.mult, after=[tend_t, tx])
        te = act.do(nc.scalar.activation, Ch[:], csB[:], ACT.Exp)
        for h in range(HPG):
            for t in range(NT):
                td = dve.do(nc.vector.tensor_scalar, csB[:, h, t * P:(t + 1) * P], csB[:, h, t * P:(t + 1) * P],
                            hcs[:, t, h:h + 1], 0.0, ALU.subtract, ALU.min, after=[te])
            td = act.do(nc.scalar.activation, csB[:, h, :], csB[:, h, :], ACT.Exp, after=[td])
            tm = dve.do(nc.vector.tensor_tensor, csB[:, h, :], csB[:, h, :], cbm[:], ALU.mult, after=[td, tcb])
            tc_ = dve.do(nc.vector.tensor_tensor, Ch[:, h, :], Ch[:, h, :], CT[:], ALU.mult, after=[te])
        ts = None
        for t in range(NT - 1):
            b_ = 3 + t % 2
            t1 = pe.do(nc.tensor.matmul, bank[b_][:, 0:2 * P], Btok[:, t * P:(t + 1) * P], xde[:, t, :], start=True,
                       stop=True, after=[tB, txe, ts])
            if t == 0:
                ts = dve.do(nc.vector.tensor_copy, ST[0][:], bank[b_][:, 0:2 * P], after=[t1])
            else:
                ts = dve.do(nc.vector.tensor_tensor, ST[t][:].rearrange("p (h c) -> p h c", h=HPG),
                            ST[t - 1][:].rearrange("p (h c) -> p h c", h=HPG),
                            dec[:, t, :].unsqueeze(2).broadcast_to([P, HPG, 64]), ALU.mult, after=[dec_t, ts])
                ts = dve.do(nc.vector.tensor_tensor, ST[t][:], ST[t][:], bank[b_][:, 0:2 * P], ALU.add, after=[t1, ts])
            yield
        pe.wait(tm, tc_, ts)
        ty = []
        for j in range(2):
            yb = bank[5 + j]
            for t in range(NT):
                cc = slice(t * P, (t + 1) * P)
                for a in range(2):
                    h = 2 * j + a
                    o = yb[64 * a:64 * a + 64, cc]
                    ins = nc.tensor.matmul(o, xdt[:, t, h * 64:(h + 1) * 64], csB[:, h, cc], start=True, stop=(t == 0))
                    if t:
                        ins = nc.tensor.matmul(o, ST[t - 1][:, h * 64:(h + 1) * 64], Ch[:, h, cc], start=False, stop=True)
                if t < NT - 1:
                    yield
            t = pe.count.mark(ins)
            t = dve.do(nc.vector.scalar_tensor_tensor, yv[j][:], xs[j][:], xbias[:, 6 + j:7 + j], yb[:], ALU.mult,
                       ALU.add, after=[t])
            t = dve.do(nc.vector.tensor_tensor, yv[j][:], yv[j][:], szs[j][:], ALU.mult, after=[t])
            ty.append(act.do(nc.scalar.activation, ysq[j][:], yv[j][:], ACT.Square, after=[t]))
            yield
        t = dve.do(nc.vector.tensor_tensor, ysq[0][:], ysq[0][:], ysq[1][:], ALU.add, after=ty)
        t = inv_rms(ysq[0][:], ysq[1], 2, 2 * P, [t])
        yield
        for j in range(2):
            t1 = dve.do(nc.vector.scalar_tensor_tensor, yv[j][:], yv[j][:], xbias[:, 4 + j:5 + j], ysq[1][:], ALU.mult,
                        ALU.mult, after=[t])
            one = ds(g * 2 + j, 1)
            to_hi_lo(yv[j][:], b_hi[:, one, :].rearrange("p a n -> p (a n)"), b_lo[:, one, :].rearrange("p a n -> p (a n)"), [t1])
        yield

    held["used4"] = held["used5"] = None
    run(ssm_products(0))
    m.loop("ssm", G - 1, lambda g: weave(ssm_mix(g), ssm_products(g + 1), 3.0))
    run(ssm_mix(G - 1))
    m.fence()

    cw = Memory(nc, work, nc.sbuf_usable_end)
    part = cw.take("part", [P, KD, T])
    aw_base = cw.at
    m_hi, m_lo = cw.take("m_hi", [P, KD, T], F32R), cw.take("m_lo", [P, KD, T], F32R)
    sgm = cw.take("sgm", [P, T])
    mval = cw.take("mval", [P, T])

    def branch(base_, w, second):
        def body(i, nxt):
            tiles = []
            for j in range(2):
                one = ds(i * 2 + j, 1)
                pk = part[:, one, :].rearrange("p a n -> p (a n)")

                def gate_evac(done, bk=2 * j):
                    held[f"bank{bk}"] = held["sig"] = act.do(nc.scalar.activation, sgm[:], bank[bk][:], ACT.Sigmoid,
                                                             after=[done, held.get("sig_used")])

                def w_evac(done, bk=2 * j + 1, one=one, pk=pk):
                    dst = mval[:] if second else pk
                    t = dve.do(nc.vector.tensor_tensor, dst, sgm[:], bank[bk][:], ALU.mult,
                               after=[done, held["sig"], held.get("mval_used")])
                    held[f"bank{bk}"] = held["sig_used"] = t
                    if second:
                        t = dve.do(nc.vector.tensor_tensor, mval[:], mval[:], pk, ALU.add, after=[t])
                        held["mval_used"] = to_hi_lo(mval[:], m_hi[:, one, :].rearrange("p a n -> p (a n)"),
                                                     m_lo[:, one, :].rearrange("p a n -> p (a n)"), [t])
                tiles += [wtile(win2[:, ds(base_ + i * 2 * P + j * P, P)], a_in, 2 * j, gate_evac),
                          wtile(w[0][:, ds(i * 2 * P + j * P, P)], b_in, 2 * j + 1, w_evac)]
            return dense(tiles, nxt)
        return body

    ssm_branch = branch(GS2, w_branch_ssm_2, False)
    m.loop("ssm_branch", KD // 2, lambda i: run(ssm_branch(i, KD * P)))
    m.fence()
    if stop == 2:
        return store(part)

    tw = Memory(nc, aw_base, nc.sbuf_usable_end)
    F = lambda name, shape=(P, T): tw.take("t_" + name, list(shape))
    sa = [F(f"st{j}") for j in range(4)]
    qw, kw, vtok, szz = F("q"), F("k"), F("vtok"), F("sz")
    nfB, nfM = F("nfB", (P, 2, T)), F("nfM", (P, 2, T))
    Sx = [F(f"S{j}") for j in range(3)]
    PT = [F(f"PT{j}") for j in range(2)]
    on, yo = F("on", (P, NT, P)), F("yo")
    stat = F("stat", (P, 8, 8))

    def att_products(i):
        def evac(j, bk, scale):
            def go(done):
                held[f"bank{bk}"] = held[f"st{j}"] = act.do(nc.scalar.activation, sa[j][:], bank[bk][:], ACT.Copy,
                                                            scale=scale, after=[done, held.get(f"used{j}")])
            return go
        return dense([wtile(win2[:, ds(b_ + i * P, P)], a_in, j % 2, evac(j, j % 2, 0.125 if j == 0 else 1.0))
                      for j, b_ in enumerate((Q2, K2, V2, ZA2))], KD * P)

    def att_mix(i):
        before = m.all_now()
        for e in (act, dve, pool):
            e.wait(*before)
        rows_t = rows_in.mark(nc.scalar.dma_start(
            nfB[:], scratch[ds(i * 2 + NFROW, 2), :].partition_broadcast(P)), 16)
        tq = dve.do(nc.vector.tensor_copy, qw[:], sa[0][:], after=[held["st0"]])
        tk = dve.do(nc.vector.tensor_copy, kw[:], sa[1][:], after=[held["st1"]])
        tz = act.do(nc.scalar.activation, szz[:], sa[3][:], ACT.Silu, after=[held["st3"]])
        held["used0"], held["used1"], held["used3"] = tq, tk, tz
        pe.wait(*before)
        for t in range(NT):
            cc = slice(t * P, (t + 1) * P)
            ins = nc.tensor.transpose(bank[2][:, cc], sa[2][:, cc], ident[:])
        t = held["used2"] = pe.count.mark(ins)
        tvt = act.do(nc.scalar.activation, vtok[:], bank[2][:], ACT.Copy, after=[t])
        for a in range(2):
            tnf = dve.do(nc.vector.tensor_tensor, v3(nfM[:, a, :]), v3(nfB[:, a, :]), across(negmask[:]), ALU.add,
                         after=[rows_t])
        yield
        units = [(a, qb) for a in range(2) for qb in range(NT)]
        sread, exped, ptread, pvread = {}, {}, {}, None

        def scores(u):
            a, qb = units[u]
            n = (qb + 1) * P
            rows_ = slice(64 * a, 64 * a + 64)
            b_ = bank[3 + u % 2]
            S = Sx[u % 3]
            t = pe.do(nc.tensor.matmul, b_[:, 0:n], qw[rows_, qb * P:n], kw[rows_, 0:n], start=True, stop=True,
                      after=[tq, tk, sread.get(u - 2)])
            st = stat[:, u, :]
            dve.do(nc.vector.memset, st[:, 6:7] if qb else st[:, 1:2], NEG, after=[t, tnf, ptread.get(u - 3)])
            t = dve.do(nc.vector.tensor_tensor_reduce, S[:, qb * P:n], b_[:, qb * P:n], nfM[:, a, qb * P:n], 1.0, NEG,
                       ALU.add, ALU.max, st[:, 0:1])
            if qb:
                t = dve.do(nc.vector.tensor_tensor_reduce, S[:, 0:qb * P], b_[:, 0:qb * P], nfB[:, a, 0:qb * P], 1.0, NEG,
                           ALU.add, ALU.max, st[:, 1:2])
            sread[u] = t
            t = dve.do(nc.vector.tensor_scalar, st[:, 2:3], st[:, 0:1], st[:, 1:2], -1.0, ALU.max, ALU.mult, after=[t])
            t = act.do(nc.scalar.activation, S[:, 0:n], S[:, 0:n], ACT.Exp, bias=st[:, 2:3], accum_out=st[:, 3:4], after=[t])
            dve.do(nc.vector.reciprocal, st[:, 4:5], st[:, 3:4], after=[t])
            exped[u] = t

        scores(0)
        yield
        copied = {}
        for u, (a, qb) in enumerate(units):
            if u + 1 < len(units):
                scores(u + 1)
                yield
            pb_ = bank[5 + u % 2]
            pe.wait(exped[u], copied.get(u - 2))
            for kb_ in range(qb + 1):
                ins = nc.tensor.transpose(pb_[:, kb_ * P:(kb_ + 1) * P], Sx[u % 3][:, kb_ * P:(kb_ + 1) * P], ident[:])
            t = ptread[u] = pe.count.mark(ins)
            n = (qb + 1) * P
            copied[u] = t = act.do(nc.scalar.activation, PT[u % 2][:, 0:n], pb_[:, 0:n], ACT.Copy, after=[t])
            yield
            pe.wait(t, tvt, pvread)
            for kb_ in range(qb + 1):
                ins = nc.tensor.matmul(bank[7][:, 0:64], PT[u % 2][:, kb_ * P:(kb_ + 1) * P],
                                       vtok[:, kb_ * P + a * 64:kb_ * P + a * 64 + 64], start=(kb_ == 0), stop=(kb_ == qb))
            t = pe.count.mark(ins)
            pvread = dve.do(nc.vector.tensor_scalar, on[:, qb, a * 64:a * 64 + 64], bank[7][:, 0:64], stat[:, u, 4:5], None,
                            ALU.mult, after=[t])
        yield
        pe.wait(pvread)
        for t in range(NT):
            ins = nc.tensor.transpose(bank[2][:, t * P:(t + 1) * P], on[:, t, :], ident[:])
        t = pe.count.mark(ins)
        t = dve.do(nc.vector.tensor_tensor, yo[:], szz[:], bank[2][:], ALU.mult, after=[t])
        one = ds(i, 1)
        to_hi_lo(yo[:], b_hi[:, one, :].rearrange("p a n -> p (a n)"), b_lo[:, one, :].rearrange("p a n -> p (a n)"), [t])
        yield

    for j in range(4):
        held[f"used{j}"] = None
    run(att_products(0))
    m.loop("attention", HS // 2 - 1, lambda i: weave(att_mix(i), att_products(i + 1), 1.4))
    run(att_mix(HS // 2 - 1))
    m.fence()
    held["sig_used"] = held["mval_used"] = None
    att_branch = branch(GA2, w_branch_att_2, True)
    m.loop("att_branch", KD // 2, lambda i: run(att_branch(i, KD * P)))
    m.fence()

    fin = nc.alloc_sbuf_tensor_at("fin", [P, KD, T], F32, offset=fin_at)

    def out_evac(mt, bk):
        def go(done):
            t = dve.do(nc.vector.tensor_copy, fin[:, mt, :], bank[bk][:], after=[done])
            held[f"bank{bk}"] = t
            held["sum"] = squares(mt, fin[:, mt, :], [sq2[0][:], sq2[1][:]], acc[:], [t])
        return go

    held["acc"] = held["sq0"] = held["sq1"] = None
    run(dense([wtile(w_out_2[0][:, mt * P:(mt + 1) * P], lambda k: (m_hi[:, k, :], m_lo[:, k, :]), mt % 2,
                     out_evac(mt, mt % 2)) for mt in range(KD)], 0))
    rt = inv_rms(acc[:], rstd, 2, D, [held["sum"]])
    for k in range(KD):
        t = dve.do(nc.vector.scalar_tensor_tensor, fin[:, k, :], fin[:, k, :], col_a[:, POST + k:POST + k + 1], rstd[:],
                   ALU.mult, ALU.mult, after=[rt])
        dve.do(nc.vector.tensor_tensor, fin[:, k, :], fin[:, k, :], xT[:, k, :], ALU.add, after=[t])
    store(fin)


_INS = ["x", "c", "w_ada", "b_ada", "norm1_w", "w_in", "conv_qkv_w", "A_log", "dt_bias", "gdn_norm_w",
        "conv_short_w", "w_out", "norm2_w", "w_gate", "w_up", "w_down", "norm_f_w", "pre_norm_g_2", "w_in_2",
        "conv_w_2", "conv_b_2", "dt_bias_2", "a_log_2", "d_skip_2", "ssm_norm_g_2", "fgate_b_2",
        "w_branch_ssm_2", "w_branch_att_2", "w_out_2", "post_norm_g_2"]
STOP = 0


def kernel(**inputs):
    import numpy as np
    import concourse.bacc as bacc
    from concourse.bass_utils import run_bass_kernel_spmd as run

    arrays = {f"in_{name}": np.ascontiguousarray(inputs[name]) for name in _INS}
    learned = {}
    for _ in range(2):
        nc = bacc.Bacc("TRN2", target_bir_lowering=False, num_devices=1)
        args = [nc.dram_tensor(n, a.shape, mybir.dt.from_np(a.dtype), kind="ExternalInput").ap()
                for n, a in arrays.items()]
        args.append(nc.dram_tensor("out", inputs["x"].shape, F32, kind="ExternalOutput").ap())
        program(nc, learned, STOP, *args)
    r = run(nc, [arrays], core_ids=[0])
    return r.results[0]["out"]
```

```python
import concourse.bass as bass
from concourse import mybir

F32 = mybir.dt.float32
F32R = mybir.dt.float32r
ALU = mybir.AluOpType
ACT = mybir.ActivationFunctionType
AX = mybir.AxisListType
ds = bass.ds

P = 128
T = 512
NT = T // P
D = 1024
KD = D // P
DFF = 2816
KF = DFF // P
KH = KF // 2
HG = 4
HS = 16
G = 4
HPG = HS // G
NEG = -1.0e30
L2_EPS = 1e-6
RMS_EPS = 1e-6

Q1, K1, V1, Z1, AB1 = 0, 512, 1024, 1536, 2048
SCB1, SCC1, SCH1 = 2056, 2568, 3080
Z2, XBC2, DT2, Q2, K2, V2, F2, ZA2, GS2, GA2 = 0, 1024, 3072, 3088, 4112, 5136, 6160, 6176, 7200, 8224

BADA, CVEC, N1, N2, NF, PRE, POST, SSMG, CB, GN = 0, 48, 56, 64, 72, 80, 88, 96, 104, 120
CQKV, CSC, CX = 0, 48, 60

CSROW, NFROW = 16, 32
SHIFT1, SCALE1, GATE1, SHIFT2, SCALE2, GATE2 = 0, 8, 16, 24, 32, 40


class Count:

    def __init__(self, nc, name):
        self.name, self.sem = name, nc.alloc_semaphore(name)
        self.n, self.per, self.reg = 0, 0, None

    def mark(self, ins, by=1):
        ins.then_inc(self.sem, by)
        self.n += by
        return (self, self.n)

    def now(self):
        return (self, self.n)


class Engine:

    def __init__(self, nc, eng, name):
        self.eng, self.count, self.seen = eng, Count(nc, name), {}

    def wait(self, *tickets):
        for t in tickets:
            if t is None:
                continue
            c, n = t
            if self.seen.get(c.name, 0) >= n:
                continue
            self.seen[c.name] = n
            self.eng.wait_ge(c.sem, n + c.reg * c.per if c.per else n)

    def do(self, fn, *args, after=(), **kw):
        self.wait(*after)
        return self.count.mark(fn(*args, **kw))

    def now(self):
        return self.count.now()


class Machine:
    def __init__(self, nc, learned):
        self.nc, self.learned = nc, learned
        self.pe = Engine(nc, nc.tensor, "pe")
        self.act = Engine(nc, nc.scalar, "act")
        self.dve = Engine(nc, nc.vector, "dve")
        self.pool = Engine(nc, nc.gpsimd, "pool")
        self.sp = Engine(nc, nc.sync, "sp")
        self.tiles = Count(nc, "tiles_done")
        self.loaded = [Count(nc, f"raw_loaded{s}") for s in range(RAW)]
        self.released = [Count(nc, f"raw_released{s}") for s in range(RAW)]
        self.hi_done = [Count(nc, f"hi_done{s}") for s in range(2)]
        self.extra = []
        self.held = {}

    def counts(self):
        return [e.count for e in (self.pe, self.act, self.dve, self.pool, self.sp)] + [self.tiles] + \
            self.loaded + self.released + self.hi_done + self.extra

    def count(self, name):
        c = Count(self.nc, name)
        self.extra.append(c)
        return c

    def compute(self):
        return (self.pe, self.act, self.dve, self.pool)

    def all_now(self):
        return [c.now() for c in self.extra if c.name == "scratch_written" and c.n] + [self.pe.now(), self.act.now(), self.dve.now(), self.pool.now(), self.tiles.now()]

    def fence(self):
        now = self.all_now()
        for e in self.compute():
            e.wait(*now)

    def loop(self, name, turns, body):
        base = {c.name: c.n for c in self.counts()}
        before = dict(self.held)
        if name not in self.learned:
            body(0)
            per = {c.name: c.n - base[c.name] for c in self.counts()}
            ends = {k: (t[0].name, t[1] - base[t[0].name]) for k, t in self.held.items() if before.get(k) != t}
            for c in self.counts():
                c.n = base[c.name] + per[c.name] * turns
            self.learned[name] = (per, ends)
            for e in (*self.compute(), self.sp):
                e.seen = {}
            return
        per, ends = self.learned[name]
        by_name = {c.name: c for c in self.counts()}
        for k, (cname, off) in ends.items():
            c, pre = by_name[cname], before.get(k)
            carried = base[cname] + off - per[cname]
            if pre is not None and not (pre[0] is c and pre[1] <= carried):
                for e in self.compute():
                    e.wait(pre)
            self.held[k] = (c, carried) if carried > 0 else None
        with self.nc.Fori(0, turns) as i:
            for c in self.counts():
                c.per, c.reg = per[c.name], i
            for e in (*self.compute(), self.sp):
                e.seen = {}
            body(i)
        for c in self.counts():
            assert c.n - base[c.name] == per[c.name], (name, c.name)
            c.n, c.per, c.reg = base[c.name] + per[c.name] * turns, 0, None
        for e in (*self.compute(), self.sp):
            e.seen = {}
        for k, (cname, off) in ends.items():
            self.held[k] = (by_name[cname], base[cname] + off + per[cname] * (turns - 1))


RAW = 4
SLOT = KH * P


class Memory:

    def __init__(self, nc, base, end):
        self.nc, self.at, self.end, self.n = nc, base, end, 0

    def take(self, name, shape, dtype=F32):
        size = 4
        for s in shape[1:]:
            size *= s
        off, self.at = self.at, self.at + (size + 31) // 32 * 32
        assert self.at <= self.end, (name, self.at, self.end)
        return self.nc.alloc_sbuf_tensor_at(name, shape, dtype, offset=off)


def program(nc, learned, stop, x, c, w_ada, b_ada, norm1_w, w_in, conv_qkv_w, A_log, dt_bias, gdn_norm_w,
            conv_short_w, w_out, norm2_w, w_gate, w_up, w_down, norm_f_w, pre_norm_g_2, w_in_2,
            conv_w_2, conv_b_2, dt_bias_2, a_log_2, d_skip_2, ssm_norm_g_2, fgate_b_2,
            w_branch_ssm_2, w_branch_att_2, w_out_2, post_norm_g_2, out):
    m = Machine(nc, learned)
    pe, act, dve, pool, sp = m.pe, m.act, m.dve, m.pool, m.sp
    held = m.held
    base = (nc.sbuf_base + 31) // 32 * 32
    mem = Memory(nc, base, nc.sbuf_usable_end)

    xT = mem.take("xT", [P, KD, T])
    fin_at = mem.at
    a_hi = mem.take("a_hi", [P, KD, T], F32R)
    a_lo = mem.take("a_lo", [P, KD, T], F32R)
    raw = [mem.take(f"raw{s}", [P, SLOT]) for s in range(RAW)]
    w_hi = [mem.take(f"w_hi{s}", [P, SLOT], F32R) for s in range(2)]
    w_lo = [mem.take(f"w_lo{s}", [P, SLOT], F32R) for s in range(2)]
    ident = mem.take("ident", [P, P])
    ones = mem.take("ones", [P, P])
    causal = mem.take("causal", [P, P])
    strict = mem.take("strict", [P, P])
    negmask = mem.take("negmask", [P, P])
    LEVELS = 7
    level = [mem.take(f"level{s}", [P, P]) for s in range(LEVELS)]
    col_a = mem.take("col_a", [P, P])
    col_b = mem.take("col_b", [P, P])
    col_d = mem.take("col_d", [P, KD])
    mod = mem.take("mod", [P, 48])
    cact = mem.take("cact", [P, KD])
    gain1 = mem.take("gain1", [P, KD])
    gain2 = mem.take("gain2", [P, KD])
    eps = mem.take("eps", [P, 1])
    gcols = mem.take("gcols", [P, NT, 8])
    bcols = mem.take("bcols", [P, NT, 8])
    dtcols = mem.take("dtcols", [P, NT, HS])
    cscols = mem.take("cscols", [P, NT, HS])
    chain = [mem.take(f"chain{i}", [P, P]) for i in range(2)]
    norm_col = mem.take("norm_col", [P, 5 * NT])
    rowc = mem.take("rowc", [P, 8])
    work = mem.at
    half = Memory(nc, work, nc.sbuf_usable_end)
    hid_hi = half.take("hid_hi", [P, KF, T], F32R)
    hid_lo = half.take("hid_lo", [P, KF, T], F32R)
    mlp = half
    mem_b = Memory(nc, work, nc.sbuf_usable_end)
    b_hi = mem_b.take("b_hi", [P, KD, T], F32R)
    b_lo = mem_b.take("b_lo", [P, KD, T], F32R)
    work = mem_b.at

    bank = [nc.alloc_psum_tensor(f"bank{i}", [P, T], F32) for i in range(8)]

    def v3(t, a=NT):
        return t.rearrange("p (a n) -> p a n", a=a)

    def across(t, n=NT):
        return t.unsqueeze(1).broadcast_to([P, n, P])

    def along(t, n=P):
        return t.unsqueeze(2).broadcast_to([P, t.shape[1], n])

    pair_in = m.count("pair_in")
    x_in = m.count("x_in")

    def load(tiles):
        nc.disable_value_cache = True
        for j, t in enumerate(tiles):
            s = j % RAW
            sp.wait((m.released[s], m.loaded[s].n // 16) if m.loaded[s].n else None)
            dst = raw[s][:, 0:t["nk"] * t["n"]].rearrange("p (k n) -> p k n", n=t["n"])
            with nc.allow_non_contiguous_dma(reason="the few columns of the decay projections"):
                if t.get("pairs") is not None:
                    nc.sync.dma_start(dst[:, :, 0:32], t["pairs"][0]).then_inc(pair_in.sem, 16)
                    dst, src = dst[:, :, 32:64], t["pairs"][1]
                else:
                    src = t["src"].rearrange("(k p) n -> p k n", p=P)
                m.loaded[s].mark(nc.sync.dma_start(dst, src), 16)
        nc.disable_value_cache = False

    def split(s, q, size):
        need = 16 * (m.released[s].n + 1)
        act.wait((m.loaded[s], need), m.tiles.now())
        hi = m.hi_done[q].mark(nc.scalar.activation(w_hi[q][:, 0:size], raw[s][:, 0:size], ACT.Copy))
        dve.wait(hi, m.tiles.now())
        held[f"pair{q}"] = m.released[s].mark(nc.vector.tensor_tensor(
            w_lo[q][:, 0:size], raw[s][:, 0:size], w_hi[q][:, 0:size].bitcast(F32), ALU.subtract))

    def dense(tiles, nxt, k_after=None):
        load(tiles)
        splits = [j for j, t in enumerate(tiles) if not t.get("plain")]
        waiting, plain, trail = [], 0, []

        def evac(t, done):
            for _ in trail.pop() if trail else ():
                pass
            steps = t["evac"](done) if t.get("evac") else None
            if steps is not None:
                trail.append(steps)
                next(steps, None)


        def column_sum(t, ready, c_):
            held[f"chain{c_}"] = done = pe.do(nc.tensor.matmul, t["out"], chain[c_][:], ones[:, 0:1], start=True, stop=True,
                                              after=[ready, held.get(f"bank{t['bank']}")])
            if t.get("evac"):
                t["evac"](done)

        for j, t in enumerate(tiles):
            s, o, n = j % RAW, t["out"], t["n"]
            bk = t["bank"]
            if t.get("direct"):
                pe.wait((m.loaded[s], 16 * (m.released[s].n + 1)), held.get(f"bank{bk}"))
                for k in range(t["nk"]):
                    ins = nc.tensor.matmul(o, raw[s][:, k * n:(k + 1) * n], t["x"](k), start=(k == 0),
                                           stop=(k == t["nk"] - 1))
                m.released[s].mark(ins)
            elif t.get("plain"):
                if waiting:
                    column_sum(*waiting.pop())
                scaled, c_ = chain[plain % 2], plain % 2
                tt = dve.do(nc.vector.tensor_scalar, scaled[:], raw[s][:, 0:n], t["x"](0), None, ALU.mult,
                            after=[(m.loaded[s], 16 * (m.released[s].n + 1)), held.get(f"chain{c_}")])
                for k in range(1, t["nk"]):
                    dve.wait(tt)
                    ins = nc.vector.scalar_tensor_tensor(scaled[:], raw[s][:, k * n:(k + 1) * n], t["x"](k), scaled[:],
                                                         ALU.mult, ALU.add)
                    tt = dve.count.mark(ins) if k < t["nk"] - 1 else m.released[s].mark(ins)
                waiting.append((t, tt, c_))
                plain += 1
            if t.get("plain"):
                if waiting and j == len(tiles) - 1:
                    column_sum(*waiting.pop())
                yield
                continue
            at = splits.index(j)
            q = at % 2
            late = False
            if at + 1 < len(splits):
                j2 = splits[at + 1]
                split(j2 % RAW, (at + 1) % 2, tiles[j2]["nk"] * tiles[j2]["n"])
            elif nxt:
                late = (at + 1) % 2 == 1
                if not late:
                    split(0, 0, nxt)
            pe.wait(held[f"pair{q}"] , held.get(f"bank{bk}"))
            for k in range(t["nk"]):
                hi_k, lo_k = w_hi[q][:, k * n:(k + 1) * n], w_lo[q][:, k * n:(k + 1) * n]
                x_hi, x_lo = t["x"](k)
                if k_after and j == 0:
                    pe.wait(k_after[k])
                first, last = k == 0 and t.get("start", True), k == t["nk"] - 1 and t.get("stop", True)
                nc.tensor.matmul(o, hi_k, x_hi, start=first, stop=False)
                nc.tensor.matmul(o, hi_k, x_lo, start=False, stop=False)
                ins = nc.tensor.matmul(o, lo_k, x_hi, start=False, stop=last)
                if k < t["nk"] - 1:
                    if trail:
                        next(trail[0], None)
                    yield
            done = m.tiles.mark(ins)
            if waiting and j == len(tiles) - 1:
                column_sum(*waiting.pop())
            if late:
                split(0, 0, nxt)
            evac(t, done)
            if j == len(tiles) - 1 and trail:
                for _ in trail.pop():
                    pass
            yield

    def queued(name):
        assert held[name], name
        return held[name]

    def run(gen):
        for _ in gen:
            pass

    def weave(mixer, products, ratio):
        due = 0.0
        for weight in mixer:
            due += ratio * (weight or 1)
            while due >= 1:
                next(products, None)
                due -= 1
        run(products)

    def a_in(k):
        return a_hi[:, k, :], a_lo[:, k, :]

    def b_in(k):
        return b_hi[:, k, :], b_lo[:, k, :]

    def wtile(src, xs, bk, evac, nk=KD, n=P, **kw):
        return dict(src=src, nk=nk, n=n, x=xs, bank=bk, out=bank[bk][0:n, :], evac=evac, **kw)

    def to_hi_lo(value, hi, lo, after):
        t_hi = act.do(nc.scalar.activation, hi, value, ACT.Copy, after=after)
        return dve.do(nc.vector.tensor_tensor, lo, value, hi.bitcast(F32), ALU.subtract, after=[t_hi, *after])

    def conv(src, acc, taps, after):
        t = dve.do(nc.vector.tensor_scalar, acc[:, :], src[:, :], taps[-1], None, ALU.mult, after=after)
        for s in range(1, len(taps)):
            yield
            t = dve.do(nc.vector.scalar_tensor_tensor, acc[:, s:T], src[:, 0:T - s], taps[-1 - s], acc[:, s:T],
                       ALU.mult, ALU.add, after=[t])
        return t

    t0 = pool.do(nc.gpsimd.memset, ident[:], 0.0)
    ones_t = pool.do(nc.gpsimd.memset, ones[:], 1.0)
    eps_t = pool.do(nc.gpsimd.memset, eps[:], RMS_EPS)
    norm_c = pool.do(nc.gpsimd.memset, norm_col[:, 4 * NT:5 * NT], -0.5)
    tn = pool.do(nc.gpsimd.memset, negmask[:], 0.0)
    ident_t = pool.do(nc.gpsimd.affine_select, out=ident[:], in_=ident[:], compare_op=ALU.not_equal, fill=1.0,
                      base=0, pattern=[[-1, P]], channel_multiplier=1, after=[tn])
    zero_rows = pool.do(nc.gpsimd.memset, rowc[:], 0.0)
    pool.do(nc.gpsimd.affine_select, out=causal[:], in_=ones[:], compare_op=ALU.is_ge, fill=0.0,
            base=0, pattern=[[1, P]], channel_multiplier=-1)
    pool.do(nc.gpsimd.affine_select, out=strict[:], in_=ones[:], compare_op=ALU.is_ge, fill=0.0,
            base=-1, pattern=[[1, P]], channel_multiplier=-1)
    masks_t = pool.do(nc.gpsimd.affine_select, out=negmask[:], in_=negmask[:], compare_op=ALU.is_ge, fill=NEG,
                      base=0, pattern=[[-1, P]], channel_multiplier=1)
    for s in range(LEVELS):
        h = 1 << s
        nb = P // (2 * h)
        v = level[s][:].rearrange("p (b e) -> p b e", b=nb)
        t = pool.do(nc.gpsimd.memset, level[s][:], 0.0)
        t = pool.do(nc.gpsimd.memset, v[:, :, h:2 * h], 1.0, after=[t])
        t = pool.do(nc.gpsimd.affine_select, out=v, in_=v, compare_op=ALU.is_ge, fill=0.0, base=0,
                    pattern=[[-2 * h, nb], [0, 2 * h]], channel_multiplier=1, after=[t])
        masks_t = pool.do(nc.gpsimd.affine_select, out=v, in_=v, compare_op=ALU.is_ge, fill=0.0, base=h - 1,
                          pattern=[[2 * h, nb], [0, 2 * h]], channel_multiplier=-1, after=[t])

    setup = Memory(nc, work, nc.sbuf_usable_end)
    xt = setup.take("x_tokens", [P, NT, D])
    pack_a = setup.take("pack_a", [P, P])
    pack_b = setup.take("pack_b", [P, P])
    pack_d = setup.take("pack_d", [P, P])
    skip2 = setup.take("skip2", [KD, 2])
    su_sq = [setup.take(f"su_sq{i}", [P, T]) for i in range(2)]
    su_acc = setup.take("su_acc", [P, T])
    su_rstd = setup.take("su_rstd", [P, T])
    su_h = [setup.take(f"su_h{i}", [P, T]) for i in range(2)]
    vec_in = m.count("vec_in")

    def rows(v):
        return v.rearrange("a (t p) -> (a t) p", p=P) if len(v.shape) == 2 else v.rearrange("(t p) -> t p", p=P)

    for t in range(NT):
        x_in.mark(nc.sync.dma_start(xt[:, t, :], x[0, t * P:(t + 1) * P, :]), 16)
    for pack, at, v in ((pack_a, CVEC, c), (pack_a, BADA, b_ada), (pack_a, N1, norm1_w), (pack_a, N2, norm2_w),
                        (pack_a, NF, norm_f_w), (pack_a, PRE, pre_norm_g_2), (pack_a, POST, post_norm_g_2),
                        (pack_a, SSMG, ssm_norm_g_2), (pack_a, CB, conv_b_2), (pack_a, GN, gdn_norm_w),
                        (pack_b, CQKV, conv_qkv_w[0]), (pack_b, CSC, conv_short_w[0]), (pack_b, CX, conv_w_2[0])):
        r = rows(v)
        vec_in.mark(nc.scalar.dma_start(pack[at:at + r.shape[0], :], r), 16)
    with nc.allow_non_contiguous_dma(reason="a few dozen numbers, one per head"):
        vec_in.mark(nc.scalar.dma_start(skip2[:], d_skip_2[0].rearrange("(t h) -> t h", h=2)), 16)
        act.wait(zero_rows)
        for col, at, v in ((0, 0, dt_bias[0]), (1, 0, A_log[0]), (2, 0, dt_bias_2[0]), (3, 0, a_log_2[0]),
                           (4, 32, fgate_b_2[0])):
            vec_in.mark(nc.scalar.dma_start(rowc[at:at + v.shape[0], col:col + 1], v.unsqueeze(1)), 16)
    vec_t = vec_in.now()

    skip_t = dve.do(nc.vector.tensor_copy, pack_d[0:KD, :].rearrange("t (h p) -> t h p", h=2),
                    skip2[:].unsqueeze(2).broadcast_to([KD, 2, P // 2]), after=[vec_t])
    pe.wait(ident_t, vec_t, skip_t)
    for b_, pack, n, col in ((0, pack_a, GN + 1, col_a), (1, pack_b, CX + 64, col_b), (2, pack_d, KD, col_d)):
        t = pe.do(nc.tensor.transpose, bank[b_][:, 0:n], pack[0:n, :], ident[0:n, 0:n])
        cols_t = dve.do(nc.vector.tensor_copy, col[:, 0:n], bank[b_][:, 0:n], after=[t])
        held[f"bank{b_}"] = cols_t
    cact_t = act.do(nc.scalar.activation, cact[:], col_a[:, CVEC:CVEC + KD], ACT.Silu, after=[cols_t])

    def squares(k, src, sq, acc, after):
        if k == 0:
            return act.do(nc.scalar.activation, acc, src, ACT.Square, after=[held.get("acc"), *after])
        t = act.do(nc.scalar.activation, sq[k % 2], src, ACT.Square, after=[held.get(f"sq{k % 2}"), *after])
        t = dve.do(nc.vector.tensor_tensor, acc, acc, sq[k % 2], ALU.add, after=[t, held["sum"]])
        held[f"sq{k % 2}"] = t
        return t

    pe.wait(*[(x_in, 64)])
    for k in range(KD):
        b_ = 3 + k % 4
        pe.wait(held.get(f"bank{b_}"))
        for t in range(NT):
            ins = nc.tensor.transpose(bank[b_][:, t * P:(t + 1) * P], xt[:, t, k * P:(k + 1) * P], ident[:])
        t = pe.count.mark(ins)
        t = dve.do(nc.vector.tensor_copy, xT[:, k, :], bank[b_][:], after=[t])
        held[f"bank{b_}"] = t
        held["sum"] = squares(k, xT[:, k, :], [su_sq[0][:], su_sq[1][:]], su_acc[:], [t])

    def inv_rms_cols(acc, bk, n, after, eps_=RMS_EPS, c=0):
        cols_in, cols_out = norm_col[:, 2 * c * NT:(2 * c + 1) * NT], norm_col[:, (2 * c + 1) * NT:(2 * c + 2) * NT]
        pe.wait(held.get(f"bank{bk}"), *after)
        for t in range(NT):
            ins = nc.tensor.matmul(bank[bk][:, t:t + 1], acc[:, t * P:(t + 1) * P], ones[:, 0:1], start=True, stop=True)
        t = pe.count.mark(ins)
        t = dve.do(nc.vector.tensor_scalar, cols_in, bank[bk][:, 0:NT], 1.0 / n, eps_, ALU.mult, ALU.add, after=[t])
        return pool.do(nc.gpsimd.tensor_tensor, cols_out, cols_in, norm_col[:, 4 * NT:5 * NT], ALU.pow,
                       after=[t, norm_c, pool.now()])

    def spread(rstd, bk, after, c=0):
        pe.wait(*after)
        for k in range(NT):
            o = (2 * c + 1) * NT + k
            ins = nc.tensor.matmul(bank[bk][:, k * P:(k + 1) * P], norm_col[:, o:o + 1].broadcast_to([P, P]),
                                   ident[:], start=True, stop=True)
        t = pe.count.mark(ins)
        t = act.do(nc.scalar.activation, rstd[:], bank[bk][:], ACT.Copy, after=[t])
        held[f"bank{bk}"] = t
        return t

    def inv_rms(acc, rstd, bk, n, after, eps_=RMS_EPS):
        return spread(rstd, bk, [inv_rms_cols(acc, bk, n, after, eps_)])

    def apply_norm(src, rstd, gain, shift, tmp, after):
        out_t = []
        for k in range(KD):
            h = tmp[k % 2]
            t = dve.do(nc.vector.scalar_tensor_tensor, h, src[:, k, :], gain[:, k:k + 1], rstd[:], ALU.mult, ALU.mult,
                       after=[held.get(f"tmp{k % 2}"), *after])
            if shift is None:
                t = to_hi_lo(h, a_hi[:, k, :], a_lo[:, k, :], [t])
            else:
                hi = act.do(nc.scalar.activation, a_hi[:, k, :], h, ACT.Identity, bias=shift[:, k:k + 1], after=[t])
                t = dve.do(nc.vector.scalar_tensor_tensor, a_lo[:, k, :], h, shift[:, k:k + 1],
                           a_hi[:, k, :].bitcast(F32), ALU.add, ALU.subtract, after=[hi])
            held[f"tmp{k % 2}"] = t
            out_t.append(t)
        return out_t

    def ada_tile(t0, j, bk, evac=None, direct=False):
        t = dict(src=w_ada[0][:, ds(t0 * P + j * P, P)], nk=KD, n=P, plain=True,
                 x=lambda k: cact[:, k:k + 1], bank=bk, out=bank[bk][:, j:j + 1], evac=evac,
                 direct=direct)
        return t

    def ada_evac(t0, n, bk):
        def go(done):
            held[f"bank{bk}"] = held["mod"] = dve.do(
                nc.vector.tensor_tensor, mod[:, ds(t0, n)], bank[bk][:, 0:n], col_a[:, ds(BADA + t0, n)], ALU.add,
                after=[done])
        return go

    pe.wait(cact_t)
    run(dense([ada_tile(0, j, 7, ada_evac(0, 16, 7) if j == 15 else None, direct=(j % 2 == 0))
               for j in range(16)], 0))
    mod_t = held["mod"]
    t = dve.do(nc.vector.scalar_tensor_tensor, gain1[:], mod[:, SCALE1:SCALE1 + KD], 1.0, col_a[:, N1:N1 + KD],
               ALU.add, ALU.mult, after=[mod_t])
    pe.wait(ones_t)
    act.wait(eps_t)
    rt = inv_rms(su_acc[:], su_rstd, 2, D, [held["sum"]])
    split(0, 0, KD * 8)
    h_t = apply_norm(xT, su_rstd, gain1, mod[:, SHIFT1:SHIFT1 + KD], [su_h[0][:], su_h[1][:]], [t, rt])

    scratch = nc.dram_tensor("row_scratch", [3 * HS, T], F32).ap()
    scratch_w = m.count("scratch_written")
    staged = Memory(nc, setup.at, nc.sbuf_usable_end)
    st_q, st_k, st_v = (staged.take(f"st_{n}", [P, T]) for n in "qkv")
    hconv, sconv = staged.take("hconv", [P, 3, 4]), staged.take("sconv", [P, 3])
    gsm = Memory(nc, staged.at, nc.sbuf_usable_end)
    r_s = [gsm.take(f"r_s{i}", [64, T]) for i in range(3)]
    reset = gsm.take("reset", [64, T])
    r_a, r_b, r_c = (r[:, :] for r in r_s)

    def softplus(x_, y, u, r_, nrow, p0, after):
        X, Y, U = x_[p0:p0 + nrow, :], y[p0:p0 + nrow, :], u[p0:p0 + nrow, :]
        t = act.do(nc.scalar.activation, Y, X, ACT.Abs, after=after)
        t = act.do(nc.scalar.activation, Y, Y, ACT.Exp, scale=-1.0, after=[t])
        yield 3
        t = dve.do(nc.vector.tensor_scalar, U, Y, 1.0, None, ALU.add, after=[t])
        t = dve.do(nc.vector.scalar_tensor_tensor, Y, U, -1.0, Y, ALU.add, ALU.subtract, after=[t])
        R = r_[p0:p0 + nrow, :]
        t1 = dve.do(nc.vector.reciprocal, R, U, after=[t])
        yield 2
        t = dve.do(nc.vector.scalar_tensor_tensor, Y, Y, -1.0, R, ALU.mult, ALU.mult, after=[t1])
        t2 = act.do(nc.scalar.activation, U, U, ACT.Ln, after=[t])
        yield 4
        t = dve.do(nc.vector.tensor_tensor, Y, Y, U, ALU.add, after=[t2])
        return dve.do(nc.vector.scalar_tensor_tensor, Y, X, 0.0, Y, ALU.max, ALU.add, after=[t])

    def chunk_reset(nrow):
        t = pool.do(nc.gpsimd.memset, reset[0:nrow, :], 1.0)
        return pool.do(nc.gpsimd.memset, v3(reset[0:nrow, :])[:, :, 0:1], 0.0, after=[t])

    reset_t = chunk_reset(64)
    t = act.do(nc.scalar.activation, rowc[0:HS, 5:6], rowc[0:HS, 1:2], ACT.Exp, after=[vec_t])
    t = act.do(nc.scalar.activation, rowc[0:HS, 6:7], rowc[0:HS, 3:4], ACT.Exp, after=[t])
    na_t = dve.do(nc.vector.tensor_scalar, rowc[0:HS, 5:7], rowc[0:HS, 5:7], -1.0, None, ALU.mult, after=[t])

    def ab_evac(done):
        src = bank[0][0:8, :]
        t = dve.do(nc.vector.tensor_scalar, r_a[0:8, :], src, rowc[0:8, 0:1], None, ALU.add, after=[done, na_t])
        held["ab"] = held["bank0"] = act.do(nc.scalar.activation, gsb[0:8, :], src, ACT.Exp, scale=-1.0, after=[t])

    def ab_rows():
        yield 3
        t2 = t = held["ab"]
        t2 = dve.do(nc.vector.tensor_scalar, gsb[0:8, :], gsb[0:8, :], 1.0, None, ALU.add, after=[t2])
        beta_t = dve.do(nc.vector.reciprocal, gsb[0:8, :], gsb[0:8, :], after=[t2])
        yield 3
        t = yield from softplus(r_a, r_b, gsu, r_c, 8, 0, [t, t2])
        yield 2
        t = dve.do(nc.vector.tensor_scalar, r_b[0:8, :], r_b[0:8, :], rowc[0:8, 5:6], None, ALU.mult, after=[t])
        t = dve.do(nc.vector.tensor_tensor_scan, gsg[0:8, :], reset[0:8, :], r_b[0:8, :], 0.0, ALU.mult, ALU.add,
                   after=[t, reset_t])
        act.wait(t, beta_t)
        scratch_w.mark(nc.scalar.dma_start(scratch[0:4, :], gsg[0:4, :]), 16)
        scratch_w.mark(nc.scalar.dma_start(scratch[4:8, :], gsb[4:8, :]), 16)
        yield 4
        pe.wait(t, beta_t, held.get("bank2"))
        for i, s_ in enumerate((gsg, gsb)):
            for j in range(NT):
                ins = nc.tensor.transpose(bank[2][:, i * 64 + j * 8:i * 64 + j * 8 + 8], s_[0:8, j * P:(j + 1) * P],
                                          ident[0:8, 0:8])
        t = pe.count.mark(ins)
        dve.do(nc.vector.tensor_copy, gcols[:], bank[2][:, 0:32].rearrange("p (a n) -> p a n", a=NT), after=[t])
        held["bank2"] = held["gb"] = dve.do(nc.vector.tensor_copy, bcols[:],
                                            bank[2][:, 64:96].rearrange("p (a n) -> p a n", a=NT))
        yield

    gsb = gsm.take("gsb", [64, T])
    gsu = gsm.take("gsu", [64, T])
    gsg = gsm.take("gsg", [64, T])
    win1 = w_in[0]
    ab = wtile(win1[:, AB1:AB1 + 8], a_in, 0, ab_evac, n=8)
    run(dense([ab], KD * P, h_t))

    below, above = Memory(nc, work, setup.at), Memory(nc, staged.at, nc.sbuf_usable_end)

    def F(name, shape=(P, T)):
        size = 4 * T if len(shape) == 2 and shape[1] == T else 0
        return (below if size and below.at + size <= below.end else above).take(name, list(shape))

    qT, kT, vT, sz = (F(f"g_{n}") for n in ("qT", "kT", "vT", "sz"))
    kb, kbe, qd = F("kb"), F("kbe"), F("qd")
    gB, bB, eg = F("gB"), F("bB"), F("eg")
    DTi, DTs = F("DTi"), F("DTs")
    LTt, ATt = F("LT"), F("AT")
    Ms = [F(f"M{s}") for s in range(LEVELS)]
    Xf, XT, Yc = F("X"), F("XT"), F("Yc")
    kdec, vb = F("kdec"), F("vb")
    Rs, vn = F("Rs", (P, P)), F("vn", (P, P))
    Sst = [F(f"S{i}", (P, P)) for i in range(2)]
    sqA = F("sqA")
    cS, uS = F("cS"), F("uS")
    hcol = F("hcol", (P, 16))

    def gdn_tiles(i):
        def cols(base_):
            return win1[:, ds(base_ + i * P, P)]
        one = ds(i, 1)
        hc = dve.do(nc.vector.tensor_copy, hconv[:].unsqueeze(3),
                    col_b[:, CQKV:CQKV + 48].rearrange("p (j s h) -> p s j h", j=4, s=3)[:, :, :, one],
                    after=[held.get("st2")])

        def conv_evac(part, dst, bk):
            def go(done):
                held[f"bank{bk}"] = held[f"st{part}"] = yield from conv(
                    bank[bk], dst, [hconv[:, part, j:j + 1] for j in range(4)], [done, hc, held.get(f"used{part}")])
            return go

        return [wtile(cols(Q1), a_in, 0, conv_evac(0, st_q, 0)),
                wtile(cols(K1), a_in, 1, conv_evac(1, st_k, 1)),
                wtile(cols(V1), a_in, 0, conv_evac(2, st_v, 0))]

    def conv_tiles(i):
        def cols(base_):
            return win1[:, ds(base_ + i * P, P)]
        hc2 = dve.do(nc.vector.tensor_copy, sconv[:].unsqueeze(2),
                     col_b[:, CSC:CSC + 12].rearrange("p (j t) -> p j t", j=3)[:, :, ds(i, 1)], after=[held.get("u")])

        def z_evac(done):
            held["bank1"] = held["sz"] = act.do(nc.scalar.activation, sz[:], bank[1][:], ACT.Silu, after=[done])


        def c_evac(done):
            held["bank0"] = held["cS"] = act.do(nc.scalar.activation, cS[:], bank[0][:], ACT.Copy,
                                                after=[done, held.get("cS_used")])

        def h_evac(done):
            t = dve.do(nc.vector.tensor_tensor, uS[:], cS[:], bank[1][:], ALU.mult, after=[done, held["cS"]])
            held["bank1"] = t
            yield
            held["u"] = yield from conv(uS, cS, [sconv[:, j:j + 1] for j in range(3)], [t, hc2])

        def b_evac(done):
            t = dve.do(nc.vector.tensor_tensor, uS[:], cS[:], bank[0][:], ALU.mult, after=[done, held["u"]])
            held["bank0"] = t
            hi = b_hi[:, ds(i + HG, 1), :].rearrange("p a n -> p (a n)")
            lo = b_lo[:, ds(i + HG, 1), :].rearrange("p a n -> p (a n)")
            held["cS_used"] = to_hi_lo(uS[:], hi, lo, [t])

        t0 = GATE1 + i * 8
        return ([wtile(cols(Z1), a_in, 1, z_evac),
                 wtile(cols(SCC1), a_in, 0, c_evac),
                 wtile(cols(SCH1), a_in, 1, h_evac),
                 wtile(cols(SCB1), a_in, 0, b_evac)],
                [ada_tile(t0, j, 7, ada_evac(t0, 8, 7) if j == 7 else None) for j in range(8)])

    def gdn_turn(i):
        tiles, ada = conv_tiles(i)
        tiles += gdn_tiles(i + 1)
        mixed = []
        for j, t in enumerate(tiles):
            mixed += [t] + (ada[2 * j:2 * j + 2] if j < 2 else ada[j + 2:j + 3])
        return dense(mixed, KD * P)

    def gdn_last(i):
        tiles, ada = conv_tiles(i)
        return dense([t for j in range(4) for t in (tiles[j], ada[2 * j], ada[2 * j + 1])], KD * P)

    rows_in = m.count("rows_in")
    Y_, Z_, ZT_, O_, S_ = 2, 3, 4, 5, 6

    def gdn_mix(i):
        held["sz"] = None
        before = m.all_now()
        for e in (act, dve, pool):
            e.wait(*before)
        act.wait(scratch_w.now())
        rows_in.mark(nc.scalar.dma_start(gB[:], scratch[ds(i, 1), :].partition_broadcast(P).rearrange("p a n -> p (a n)")), 16)
        rows_in.mark(nc.scalar.dma_start(bB[:], scratch[ds(i + 4, 1), :].partition_broadcast(P).rearrange("p a n -> p (a n)")), 16)
        rows_t = rows_in.now()
        t = dve.do(nc.vector.tensor_copy, hcol[:, 0:NT].unsqueeze(2), gcols[:, :, ds(i, 1)])
        hc_t = dve.do(nc.vector.tensor_copy, hcol[:, NT:2 * NT].unsqueeze(2), bcols[:, :, ds(i + 4, 1)])
        st = [held[f"st{j}"] for j in range(3)]
        tq, tk = (act.do(nc.scalar.activation, dst[:], src[:], ACT.Silu, after=[s_])
                          for dst, src, s_ in ((qT, st_q, st[0]), (kT, st_k, st[1])))
        held["used0"], held["used1"] = tq, tk
        t1 = act.do(nc.scalar.activation, sqA[:], qT[:], ACT.Square, after=[tq])
        t2 = act.do(nc.scalar.activation, Yc[:], kT[:], ACT.Square, after=[tk])
        held["used2"] = tv = act.do(nc.scalar.activation, vT[:], st_v[:], ACT.Silu, after=[st[2]])
        yield 8
        pe.wait(*before)
        t1 = inv_rms_cols(sqA[:], Y_, 1, [t1], L2_EPS, c=0)
        t2 = inv_rms_cols(Yc[:], Z_, 1, [t2], L2_EPS, c=1)
        yield 5
        t1 = spread(sqA, Y_, [t1], c=0)
        t2 = spread(Yc, Z_, [t2], c=1)
        tq = dve.do(nc.vector.scalar_tensor_tensor, qT[:], qT[:], float(P) ** -0.5, sqA[:], ALU.mult, ALU.mult, after=[t1])
        tk = dve.do(nc.vector.tensor_tensor, kT[:], kT[:], Yc[:], ALU.mult, after=[t2])
        for t in range(NT):
            dt_ = dve.do(nc.vector.tensor_scalar, DTi[:, t * P:(t + 1) * P], gB[:, t * P:(t + 1) * P],
                         hcol[:, t:t + 1], 0.0, ALU.subtract, ALU.min, after=[rows_t, hc_t])
        te = act.do(nc.scalar.activation, eg[:], gB[:], ACT.Exp, after=[rows_t])
        t = act.do(nc.scalar.activation, DTi[:], DTi[:], ACT.Exp, after=[dt_])
        tkb = dve.do(nc.vector.tensor_tensor, kb[:], kT[:], bB[:], ALU.mult, after=[tk])
        tdi = dve.do(nc.vector.tensor_tensor, v3(DTs[:]), v3(DTi[:]), across(strict[:]), ALU.mult, after=[t])
        tda = dve.do(nc.vector.tensor_tensor, v3(DTi[:]), v3(DTi[:]), across(causal[:]), ALU.mult, after=[tdi])
        yield 7
        pe.wait(tkb)
        for t in range(NT):
            cc = slice(t * P, (t + 1) * P)
            ins = nc.tensor.matmul(bank[Y_][:, cc], kT[:, cc], kb[:, cc], start=True, stop=True)
        tY = pe.count.mark(ins)
        tL = dve.do(nc.vector.tensor_tensor, LTt[:], bank[Y_][:], DTs[:], ALU.mult, after=[tY, tdi])
        yield 3
        tM = []
        for s in range(LEVELS):
            tM.append(pool.do(nc.gpsimd.tensor_tensor, v3(Ms[s][:]), v3(LTt[:]), across(level[s][:]), ALU.mult,
                              after=[tL, masks_t]))
        pe.wait(tq)
        for t in range(NT):
            cc = slice(t * P, (t + 1) * P)
            ins = nc.tensor.matmul(bank[Z_][:, cc], kT[:, cc], qT[:, cc], start=True, stop=True)
        tZ = pe.count.mark(ins)
        tA = dve.do(nc.vector.tensor_tensor, ATt[:], bank[Z_][:], DTi[:], ALU.mult, after=[tZ, tda])
        tkbe = dve.do(nc.vector.tensor_tensor, kbe[:], kb[:], eg[:], ALU.mult, after=[te])
        tqd = dve.do(nc.vector.tensor_tensor, qd[:], qT[:], eg[:], ALU.mult)
        yield 3
        pe.wait(tv)
        for t in range(NT):
            cc = slice(t * P, (t + 1) * P)
            ins = nc.tensor.transpose(bank[ZT_][:, cc], kT[:, cc], ident[:])
        tkt = pe.count.mark(ins)
        for t in range(NT):
            cc = slice(t * P, (t + 1) * P)
            ins = nc.tensor.transpose(bank[O_][:, cc], vT[:, cc], ident[:])
        tvt = pe.count.mark(ins)
        glast = v3(gB[:])[:, :, P - 1:P]
        t = dve.do(nc.vector.tensor_tensor, hcol[:, 8:12].unsqueeze(2), glast, hcol[:, 0:NT].unsqueeze(2), ALU.subtract)
        t = act.do(nc.scalar.activation, hcol[:, 8:12], hcol[:, 8:12], ACT.Exp, after=[t])
        tkd = dve.do(nc.vector.tensor_tensor, v3(kdec[:]), v3(bank[ZT_][:]), along(hcol[:, 8:12]), ALU.mult, after=[tkt, t])
        tvb = dve.do(nc.vector.tensor_tensor, v3(vb[:]), v3(bank[O_][:]), along(hcol[:, 4:8]), ALU.mult, after=[tvt])
        yield 3
        pe.wait(tM[0])
        for t in range(NT):
            cc = slice(t * P, (t + 1) * P)
            ins = nc.tensor.transpose(bank[Y_][:, cc], Ms[0][:, cc], ident[:])
        tY = pe.count.mark(ins)
        tXT = dve.do(nc.vector.tensor_tensor, v3(XT[:]), across(ident[:]), v3(Ms[0][:]), ALU.subtract, after=[tM[0]])
        tX = dve.do(nc.vector.tensor_tensor, v3(Xf[:]), across(ident[:]), v3(bank[Y_][:]), ALU.subtract, after=[tY])
        yield 2
        for s in range(1, LEVELS):
            pe.wait(tX, tM[s])
            for t in range(NT):
                cc = slice(t * P, (t + 1) * P)
                ins = nc.tensor.matmul(bank[Y_][:, cc], Ms[s][:, cc], Xf[:, cc], start=True, stop=True)
            t = pe.count.mark(ins)
            tYc = act.do(nc.scalar.activation, Yc[:], bank[Y_][:], ACT.Copy, after=[t])
            yield 2
            pe.wait(tYc, tXT)
            for t in range(NT):
                cc = slice(t * P, (t + 1) * P)
                ins = nc.tensor.matmul(bank[ZT_][:, cc], Yc[:, cc], XT[:, cc], start=True, stop=True)
            tZT = pe.count.mark(ins)
            if s < LEVELS - 1:
                for t in range(NT):
                    cc = slice(t * P, (t + 1) * P)
                    ins = nc.tensor.matmul(bank[Z_][:, cc], XT[:, cc], Yc[:, cc], start=True, stop=True)
                tZ = pe.count.mark(ins)
                tX = dve.do(nc.vector.tensor_tensor, Xf[:], Xf[:], bank[Z_][:], ALU.subtract, after=[tZ])
            tXT = dve.do(nc.vector.tensor_tensor, XT[:], XT[:], bank[ZT_][:], ALU.subtract, after=[tZT, tX])
            yield 2
        tS, tvn, tO = None, None, None
        pe.wait(tXT, tkbe, tqd, tA, tkd, tvb)
        for t in range(NT):
            cc = slice(t * P, (t + 1) * P)
            S_in, S_out = Sst[(t + 1) % 2], Sst[t % 2]
            if t == 0:
                rhs = vb[:, cc]
            else:
                t1 = pe.do(nc.tensor.matmul, bank[S_][:, 0:P], kbe[:, cc], S_in[:], start=True, stop=True, after=[tS])
                t1 = dve.do(nc.vector.tensor_tensor, Rs[:], vb[:, cc], bank[S_][:, 0:P], ALU.subtract, after=[t1])
                rhs = Rs[:]
                pe.do(nc.tensor.matmul, bank[O_][:, cc], S_in[:], qd[:, cc], start=True, stop=False)
                pe.wait(t1)
                yield
            t1 = pe.do(nc.tensor.matmul, bank[S_][:, P:2 * P], XT[:, cc], rhs, start=True, stop=True)
            tvn = act.do(nc.scalar.activation, vn[:], bank[S_][:, P:2 * P], ACT.Copy, after=[t1])
            yield
            if t < NT - 1:
                t1 = pe.do(nc.tensor.matmul, bank[S_][:, 2 * P:3 * P], kdec[:, cc], vn[:], start=True, stop=True, after=[tvn])
                if t == 0:
                    tS = dve.do(nc.vector.tensor_copy, S_out[:], bank[S_][:, 2 * P:3 * P], after=[t1])
                else:
                    tS = dve.do(nc.vector.scalar_tensor_tensor, S_out[:], S_in[:], eg[:, (t + 1) * P - 1:(t + 1) * P],
                                bank[S_][:, 2 * P:3 * P], ALU.mult, ALU.add, after=[t1])
            tO = pe.do(nc.tensor.matmul, bank[O_][:, cc], vn[:], ATt[:, cc], start=(t == 0), stop=True, after=[tvn])
            yield
        t = act.do(nc.scalar.activation, sqA[:], bank[O_][:], ACT.Square, after=[tO])
        yield 2
        t = inv_rms_cols(sqA[:], Y_, P, [t])
        yield 5
        t = spread(sqA, Y_, [t])
        t = dve.do(nc.vector.scalar_tensor_tensor, Yc[:], bank[O_][:], col_a[:, GN:GN + 1], sqA[:], ALU.mult, ALU.mult, after=[t])
        t = dve.do(nc.vector.tensor_tensor, Yc[:], Yc[:], sz[:], ALU.mult, after=[t, queued("sz")])
        to_hi_lo(Yc[:], b_hi[:, ds(i, 1), :].rearrange("p a n -> p (a n)"),
                 b_lo[:, ds(i, 1), :].rearrange("p a n -> p (a n)"), [t])
        yield

    weave(ab_rows(), dense(gdn_tiles(0), KD * P), 1.0)
    m.loop("delta_net", HG - 1, lambda i: weave(gdn_mix(i), gdn_turn(i), 0.85))
    weave(gdn_mix(HG - 1), gdn_last(HG - 1), 0.6)
    m.fence()

    pw = Memory(nc, mlp.at, nc.sbuf_usable_end)
    acc = pw.take("p_acc", [P, T])
    sq2 = [pw.take(f"p_sq{i}", [P, T]) for i in range(2)]
    sgate = pw.take("p_sgate", [P, T])
    hval = pw.take("p_hval", [P, T])
    rstd, rstd1 = pw.take("p_rstd", [P, T]), pw.take("p_rstd1", [P, T])
    acc2 = hval
    tmpn = [sq2[0][:], sgate[:]]

    def residual(mt, bk, gate, weigh=None):
        def go(done):
            xk = xT[:, mt, :]
            t = dve.do(nc.vector.scalar_tensor_tensor, xk, bank[bk][:], gate[:, mt:mt + 1], xk, ALU.mult, ALU.add,
                       after=[done])
            held[f"bank{bk}"] = t
            held["sum"] = squares(mt, xk, [sq2[0][:], sq2[1][:]], acc[:], [t])
            if weigh is not None:
                w = dict(scale=weigh[:, mt:mt + 1], after=[t, held.get("sum2")])
                if mt == 0:
                    held["sum2"] = act.do(nc.scalar.activation, acc2[:], xk, ACT.Square, **w)
                else:
                    t = act.do(nc.scalar.activation, sgate[:], xk, ACT.Square, **w)
                    held["sum2"] = dve.do(nc.vector.tensor_tensor, acc2[:], acc2[:], sgate[:], ALU.add, after=[t])
        return go

    held["acc"] = held["sq0"] = held["sq1"] = None
    run(dense([wtile(w_out[0][:, mt * P:(mt + 1) * P], b_in, mt % 2, residual(mt, mt % 2, mod[:, GATE1:GATE1 + KD]))
               for mt in range(KD)], KD * P))
    t = dve.do(nc.vector.scalar_tensor_tensor, gain2[:], mod[:, SCALE2:SCALE2 + KD], 1.0, col_a[:, N2:N2 + KD],
               ALU.add, ALU.mult)
    rt = inv_rms(acc[:], rstd, 2, D, [held["sum"]])
    m.fence()
    held["tmp0"] = held["tmp1"] = None
    h_t = apply_norm(xT, rstd, gain2, mod[:, SHIFT2:SHIFT2 + KD], tmpn, [t, rt])

    def hidden(i, nxt, k_after=None):
        tiles = []
        for j in range(2):
            def gate_evac(done, bk=2 * j):
                held[f"bank{bk}"] = held["silu"] = act.do(nc.scalar.activation, sgate[:], bank[bk][:], ACT.Silu,
                                                          after=[done, held.get("silu_used")])

            def up_evac(done, bk=2 * j + 1, j=j):
                t = dve.do(nc.vector.tensor_tensor, hval[:], sgate[:], bank[bk][:], ALU.mult,
                           after=[done, held["silu"], held.get("hval_used")])
                held[f"bank{bk}"] = held["silu_used"] = t
                one = ds(i * 2 + j, 1)
                held["hval_used"] = to_hi_lo(hval[:], hid_hi[:, one, :].rearrange("p a n -> p (a n)"),
                                             hid_lo[:, one, :].rearrange("p a n -> p (a n)"), [t])
            cs = ds(i * 2 * P + j * P, P)
            tiles += [wtile(w_gate[0][:, cs], a_in, 2 * j, gate_evac), wtile(w_up[0][:, cs], a_in, 2 * j + 1, up_evac)]
        return dense(tiles, nxt, k_after)

    run(hidden(0, KD * P, h_t))
    m.loop("mlp_hidden", KF // 2 - 2, lambda i: run(hidden(i + 1, KD * P)))
    run(hidden(KF // 2 - 1, KH * P))
    m.fence()

    def down(mt, half_):
        lo_row = half_ * KH

        def x_of(k):
            return hid_hi[:, lo_row + k, :], hid_lo[:, lo_row + k, :]
        ev = residual(mt, mt % 2, mod[:, GATE2:GATE2 + KD], col_a[:, NF:NF + KD]) if half_ else None
        return wtile(w_down[0][lo_row * P:(lo_row + KH) * P, mt * P:(mt + 1) * P], x_of, mt % 2, ev, nk=KH,
                     start=(half_ == 0), stop=(half_ == 1))

    held["acc"] = held["sq0"] = held["sq1"] = None
    run(dense([down(mt, h) for mt in range(KD) for h in range(2)], 0))
    inv_rms_cols(acc[:], 2, D, [held["sum"]], c=0)
    r1 = norm_col[:, NT:2 * NT]
    in2, r2c = norm_col[:, 2 * NT:3 * NT], norm_col[:, 3 * NT:4 * NT]
    pe.wait(held["sum2"], held.get("bank3"))
    for t in range(NT):
        ins = nc.tensor.matmul(bank[3][:, t:t + 1], acc2[:, t * P:(t + 1) * P], ones[:, 0:1], start=True, stop=True)
    t = pe.count.mark(ins)
    t = dve.do(nc.vector.scalar_tensor_tensor, in2, bank[3][:, 0:NT], 1.0 / D, r1, ALU.mult, ALU.mult, after=[t, pool.now()])
    held["bank3"] = t
    t = dve.do(nc.vector.tensor_tensor, in2, in2, r1, ALU.mult, after=[t])
    t = dve.do(nc.vector.tensor_scalar, in2, in2, RMS_EPS, None, ALU.add, after=[t])
    t = pool.do(nc.gpsimd.tensor_tensor, r2c, in2, norm_col[:, 4 * NT:5 * NT], ALU.pow, after=[t])
    t12 = dve.do(nc.vector.tensor_tensor, r2c, r2c, r1, ALU.mult, after=[t])
    rt12 = spread(rstd, 2, [t12], c=1)
    rt1 = spread(rstd1, 3, [t12], c=0)
    both = dve.do(nc.vector.tensor_tensor, gain1[:], col_a[:, NF:NF + KD], col_a[:, PRE:PRE + KD], ALU.mult)

    out_c = m.count("out_stored")

    def store(src, add=None):
        m.fence()
        ow = Memory(nc, work, nc.sbuf_usable_end)
        toks = [ow.take(f"o_tok{t}", [P, D]) for t in range(NT)]
        for t in range(NT):
            for h in range(2):
                b_ = 2 * (t % 2) + h
                pe.wait(held.get(f"bank{b_}"))
                for k in range(4):
                    ins = nc.tensor.transpose(bank[b_][:, k * P:(k + 1) * P], src[:, h * 4 + k, t * P:(t + 1) * P], ident[:])
                tt = pe.count.mark(ins)
                e, fn = (act, None) if h else (dve, None)
                if h:
                    tt = act.do(nc.scalar.activation, toks[t][:, h * T:(h + 1) * T], bank[b_][:], ACT.Copy, after=[tt])
                else:
                    tt = dve.do(nc.vector.tensor_copy, toks[t][:, h * T:(h + 1) * T], bank[b_][:], after=[tt])
                held[f"bank{b_}"] = tt
                sp.wait(tt)
            out_c.mark(nc.sync.dma_start(out[0, t * P:(t + 1) * P, :], toks[t][:]), 16)
        sp.wait(out_c.now())

    m.fence()
    held["tmp0"] = held["tmp1"] = None
    sw = Memory(nc, work, nc.sbuf_usable_end)
    st2 = [sw.take(f"s_st{j}", [P, T]) for j in range(4)]
    xconv = sw.take("s_xconv", [P, 4, 4])
    r2 = Memory(nc, sw.at, nc.sbuf_usable_end)
    rx, ry, ru, rcs, rcum = (r2.take(f"r2_{n}", [64, T]) for n in ("x", "y", "u", "cs", "cum"))
    rr, reset2 = r2.take("r2_r", [64, T]), r2.take("r2_reset", [64, T])
    assert r2.at <= mlp.at
    z_t = pool.do(nc.gpsimd.memset, rx[:], 0.0)
    t = pool.do(nc.gpsimd.memset, reset2[:], 1.0)
    reset_t = pool.do(nc.gpsimd.memset, v3(reset2[:, :])[:, :, 0:1], 0.0, after=[t])

    def dtf_evac(done):
        dve.do(nc.vector.tensor_scalar, rx[0:HS, :], bank[0][0:HS, :], rowc[0:HS, 2:3], None, ALU.add, after=[done, z_t])
        t = dve.do(nc.vector.tensor_scalar, rx[32:32 + HS, :], bank[0][32:32 + HS, :], rowc[32:32 + HS, 4:5], -1.0,
                   ALU.add, ALU.mult)
        held["bank0"] = held["dtf"] = t

    def dtf_rows():
        yield 2
        t = yield from softplus(rx, ry, ru, rr, 64, 0, [held["dtf"]])
        yield 2
        t1 = dve.do(nc.vector.tensor_scalar, rcs[0:HS, :], ry[0:HS, :], rowc[0:HS, 6:7], None, ALU.mult, after=[t])
        t1 = dve.do(nc.vector.tensor_tensor_scan, rcum[0:HS, :], reset2[0:HS, :], rcs[0:HS, :], 0.0, ALU.mult, ALU.add,
                    after=[t1, reset_t])
        t2 = pool.do(nc.gpsimd.memset, rcs[32:32 + HS, :], 1.0, after=[pool.now()])
        t2 = dve.do(nc.vector.tensor_tensor_scan, rcum[32:32 + HS, :], rcs[32:32 + HS, :], ry[32:32 + HS, :], 0.0,
                    ALU.mult, ALU.add, after=[t2])
        act.wait(t1, t2)
        scratch_w.mark(nc.scalar.dma_start(scratch[CSROW:CSROW + HS, :], rcum[0:HS, :]), 16)
        scratch_w.mark(nc.scalar.dma_start(scratch[NFROW:NFROW + HS, :], rcum[32:32 + HS, :]), 16)
        yield 4
        pe.wait(t1, held.get("bank2"))
        for i, s_ in enumerate((ry, rcum)):
            for j in range(NT):
                ins = nc.tensor.transpose(bank[2][:, i * 64 + j * HS:i * 64 + j * HS + HS], s_[0:HS, j * P:(j + 1) * P],
                                          ident[0:HS, 0:HS])
        t = pe.count.mark(ins)
        dve.do(nc.vector.tensor_copy, dtcols[:], v3(bank[2][:, 0:64]), after=[t])
        held["bank2"] = dve.do(nc.vector.tensor_copy, cscols[:], v3(bank[2][:, 64:128]))
        yield

    win2 = w_in_2[0]
    dtf = wtile(None, a_in, 0, dtf_evac, n=64)
    dtf["pairs"] = [win2[:, c0:c0 + 32].rearrange("(k p) n -> p k n", p=P) for c0 in (DT2, F2)]
    act.wait((pair_in, 16))
    dve.wait((pair_in, 16))
    split(0, 0, KD * 64)
    h_t = apply_norm(xT, rstd, gain1, None, tmpn, [rt12, both])
    run(dense([dtf], KD * P, h_t))
    for k in range(KD):
        dve.do(nc.vector.scalar_tensor_tensor, xT[:, k, :], xT[:, k, :], col_a[:, NF + k:NF + k + 1], rstd1[:],
               ALU.mult, ALU.mult, after=[rt1])

    F = lambda name, shape=(P, T): sw.take("s_" + name, list(shape))
    xs = [F(f"xs{j}") for j in range(2)]
    BT, CT = F("BT"), F("CT")
    szs = [F(f"sz{j}") for j in range(2)]
    csB, Ch = F("csB", (P, HPG, T)), F("Ch", (P, HPG, T))
    cbm, Btok = F("cbm"), F("Btok")
    xdt, xde = F("xdt", (P, NT, 2 * P)), F("xde", (P, NT, 2 * P))
    ST = [F(f"ST{t}", (P, 2 * P)) for t in range(1, NT)]
    yv = [F(f"yv{j}") for j in range(2)]
    ysq = [F(f"ysq{j}") for j in range(2)]
    xbias = F("xbias", (P, 8))
    hcs, hdt, tend, dec = (F(n, (P, NT, HPG)) for n in ("hcs", "hdt", "tend", "dec"))

    def cols2(base_, g, per):
        return win2[:, ds(base_ + g * per, P)]

    def z_tiles(g):
        def z_evac(j, bk):
            def go(done):
                held[f"bank{bk}"] = held[f"sz{j}"] = act.do(nc.scalar.activation, szs[j][:], bank[bk][:], ACT.Silu,
                                                            after=[done])
            return go
        return [wtile(cols2(Z2, g, 2 * P), a_in, 0, z_evac(0, 0)), wtile(cols2(Z2 + P, g, 2 * P), a_in, 1, z_evac(1, 1))]

    def xbc_tiles(g):
        taps = col_b[:, CX:CX + 64].rearrange("p (j t) -> p t j", j=4)
        dve.wait(held.get("st3"))
        dve.do(nc.vector.tensor_copy, xconv[:, 0:2, :], taps[:, ds(g * 2, 2), :])
        dve.do(nc.vector.tensor_copy, xconv[:, 2:3, :], taps[:, ds(g + 2 * G, 1), :])
        xc = dve.do(nc.vector.tensor_copy, xconv[:, 3:4, :], taps[:, ds(g + 3 * G, 1), :])

        def conv_evac(j, bk):
            def go(done):
                held[f"bank{bk}"] = held[f"st{j}"] = yield from conv(
                    bank[bk], st2[j], [xconv[:, j, a:a + 1] for a in range(4)], [done, xc, held.get(f"used{j}")])
            return go

        BC = XBC2 + D
        return [wtile(cols2(XBC2, g, 2 * P), a_in, 0, conv_evac(0, 0)),
                wtile(cols2(XBC2 + P, g, 2 * P), a_in, 1, conv_evac(1, 1)),
                wtile(cols2(BC, g, P), a_in, 0, conv_evac(2, 0)),
                wtile(cols2(BC + G * P, g, P), a_in, 1, conv_evac(3, 1))]

    def ssm_mix(g):
        held["sz0"] = held["sz1"] = None
        before = m.all_now()
        for e in (act, dve, pool):
            e.wait(*before)
        act.wait(scratch_w.now())
        rows_t = rows_in.mark(nc.scalar.dma_start(
            csB[:], scratch[ds(g * HPG + CSROW, HPG), :].partition_broadcast(P)), 16)
        dve.do(nc.vector.tensor_copy, hcs[:], cscols[:, :, ds(g * HPG, HPG)])
        dve.do(nc.vector.tensor_copy, hdt[:], dtcols[:, :, ds(g * HPG, HPG)])
        dve.do(nc.vector.tensor_copy, xbias[:, 0:2], col_a[:, ds(g * 2 + CB, 2)])
        dve.do(nc.vector.tensor_copy, xbias[:, 2:3], col_a[:, ds(g + CB + 2 * G, 1)])
        dve.do(nc.vector.tensor_copy, xbias[:, 3:4], col_a[:, ds(g + CB + 3 * G, 1)])
        dve.do(nc.vector.tensor_copy, xbias[:, 4:6], col_a[:, ds(g * 2 + SSMG, 2)])
        xb = dve.do(nc.vector.tensor_copy, xbias[:, 6:8], col_d[:, ds(g * 2, 2)])
        tt = []
        for j, dst in enumerate((xs[0], xs[1], BT, CT)):
            tt.append(act.do(nc.scalar.activation, dst[:], st2[j][:], ACT.Silu, bias=xbias[:, j:j + 1],
                             after=[held[f"st{j}"], xb]))
            held[f"used{j}"] = tt[-1]
        yield 7
        pe.wait(*before, tt[3])
        for t in range(NT):
            cc = slice(t * P, (t + 1) * P)
            ins = nc.tensor.matmul(bank[2][:, cc], BT[:, cc], CT[:, cc], start=True, stop=True)
        t = pe.count.mark(ins)
        tcb = dve.do(nc.vector.tensor_tensor, v3(cbm[:]), v3(bank[2][:]), across(causal[:]), ALU.mult, after=[t])
        yield
        for t in range(NT):
            cc = slice(t * P, (t + 1) * P)
            ins = nc.tensor.transpose(bank[3][:, cc], BT[:, cc], ident[:])
        t = pe.count.mark(ins)
        tB = act.do(nc.scalar.activation, Btok[:], bank[3][:], ACT.Copy, after=[t])
        yield
        for u in range(2):
            for t in range(2):
                for j in range(2):
                    cc = slice((2 * u + t) * P, (2 * u + t + 1) * P)
                    ins = nc.tensor.transpose(bank[4 + u][:, t * 2 * P + j * P:t * 2 * P + (j + 1) * P], xs[j][:, cc], ident[:])
            t = pe.count.mark(ins)
            tx = dve.do(nc.vector.tensor_tensor,
                        xdt[:, 2 * u:2 * u + 2, :].rearrange("p t (h c) -> p t h c", h=HPG),
                        bank[4 + u][:].rearrange("p (t h c) -> p t h c", t=2, h=HPG),
                        hdt[:, 2 * u:2 * u + 2, :].unsqueeze(3).broadcast_to([P, 2, HPG, 64]), ALU.mult, after=[t])
            yield
        last = csB[:].rearrange("p h (t n) -> p t h n", t=NT)[:, :, :, P - 1]
        t = dve.do(nc.vector.tensor_tensor, tend[:], last, hcs[:], ALU.subtract, after=[rows_t])
        tend_t = act.do(nc.scalar.activation, tend[:], tend[:], ACT.Exp, after=[t])
        dec_t = act.do(nc.scalar.activation, dec[:], last, ACT.Exp)
        txe = dve.do(nc.vector.tensor_tensor, xde[:].rearrange("p t (h c) -> p t h c", h=HPG),
                     xdt[:].rearrange("p t (h c) -> p t h c", h=HPG),
                     tend[:].unsqueeze(3).broadcast_to([P, NT, HPG, 64]), ALU.mult, after=[tend_t, tx])
        te = act.do(nc.scalar.activation, Ch[:], csB[:], ACT.Exp)
        for h in range(HPG):
            for t in range(NT):
                td = dve.do(nc.vector.tensor_scalar, csB[:, h, t * P:(t + 1) * P], csB[:, h, t * P:(t + 1) * P],
                            hcs[:, t, h:h + 1], 0.0, ALU.subtract, ALU.min, after=[te])
            td = act.do(nc.scalar.activation, csB[:, h, :], csB[:, h, :], ACT.Exp, after=[td])
            tm = dve.do(nc.vector.tensor_tensor, csB[:, h, :], csB[:, h, :], cbm[:], ALU.mult, after=[td, tcb])
            tc_ = dve.do(nc.vector.tensor_tensor, Ch[:, h, :], Ch[:, h, :], CT[:], ALU.mult, after=[te])
            yield 3
        ts = None
        for t in range(NT - 1):
            b_ = 3 + t % 2
            t1 = pe.do(nc.tensor.matmul, bank[b_][:, 0:2 * P], Btok[:, t * P:(t + 1) * P], xde[:, t, :], start=True,
                       stop=True, after=[tB, txe, ts])
            if t == 0:
                ts = dve.do(nc.vector.tensor_copy, ST[0][:], bank[b_][:, 0:2 * P], after=[t1])
            else:
                ts = dve.do(nc.vector.tensor_tensor, ST[t][:].rearrange("p (h c) -> p h c", h=HPG),
                            ST[t - 1][:].rearrange("p (h c) -> p h c", h=HPG),
                            dec[:, t, :].unsqueeze(2).broadcast_to([P, HPG, 64]), ALU.mult, after=[dec_t, ts])
                ts = dve.do(nc.vector.tensor_tensor, ST[t][:], ST[t][:], bank[b_][:, 0:2 * P], ALU.add, after=[t1, ts])
            yield
        yield 2
        pe.wait(tm, tc_, ts)
        ty = []
        for j in range(2):
            yb = bank[5 + j]
            for t in range(NT):
                cc = slice(t * P, (t + 1) * P)
                for a in range(2):
                    h = 2 * j + a
                    o = yb[64 * a:64 * a + 64, cc]
                    ins = nc.tensor.matmul(o, xdt[:, t, h * 64:(h + 1) * 64], csB[:, h, cc], start=True, stop=(t == 0))
                    if t:
                        ins = nc.tensor.matmul(o, ST[t - 1][:, h * 64:(h + 1) * 64], Ch[:, h, cc], start=False, stop=True)
                if t < NT - 1:
                    yield
            t = pe.count.mark(ins)
            t = dve.do(nc.vector.scalar_tensor_tensor, yv[j][:], xs[j][:], xbias[:, 6 + j:7 + j], yb[:], ALU.mult,
                       ALU.add, after=[t])
            t = dve.do(nc.vector.tensor_tensor, yv[j][:], yv[j][:], szs[j][:], ALU.mult, after=[t, queued(f"sz{j}")])
            ty.append(act.do(nc.scalar.activation, ysq[j][:], yv[j][:], ACT.Square, after=[t]))
            yield
        t = dve.do(nc.vector.tensor_tensor, ysq[0][:], ysq[0][:], ysq[1][:], ALU.add, after=ty)
        yield 4
        t = inv_rms_cols(ysq[0][:], 2, 2 * P, [t])
        yield 4
        t = spread(ysq[1], 2, [t])
        for j in range(2):
            t1 = dve.do(nc.vector.scalar_tensor_tensor, yv[j][:], yv[j][:], xbias[:, 4 + j:5 + j], ysq[1][:], ALU.mult,
                        ALU.mult, after=[t])
            one = ds(g * 2 + j, 1)
            to_hi_lo(yv[j][:], b_hi[:, one, :].rearrange("p a n -> p (a n)"), b_lo[:, one, :].rearrange("p a n -> p (a n)"), [t1])
        yield

    weave(dtf_rows(), dense(xbc_tiles(0), KD * P), 1.0)
    m.loop("ssm", G - 1, lambda g: weave(ssm_mix(g), dense(z_tiles(g) + xbc_tiles(g + 1), KD * P), 1.1))
    weave(ssm_mix(G - 1), dense(z_tiles(G - 1), KD * P), 0.7)
    m.fence()

    cw = Memory(nc, work, nc.sbuf_usable_end)
    part = cw.take("part", [P, KD, T])
    aw_base = cw.at
    m_hi, m_lo = cw.take("m_hi", [P, KD, T], F32R), cw.take("m_lo", [P, KD, T], F32R)
    sgm = cw.take("sgm", [P, T])
    mval = cw.take("mval", [P, T])

    def branch(base_, w, second):
        def body(i, nxt):
            tiles = []
            for j in range(2):
                one = ds(i * 2 + j, 1)
                pk = part[:, one, :].rearrange("p a n -> p (a n)")

                def gate_evac(done, bk=2 * j):
                    held[f"bank{bk}"] = held["sig"] = act.do(nc.scalar.activation, sgm[:], bank[bk][:], ACT.Sigmoid,
                                                             after=[done, held.get("sig_used")])

                def w_evac(done, bk=2 * j + 1, one=one, pk=pk):
                    dst = mval[:] if second else pk
                    t = dve.do(nc.vector.tensor_tensor, dst, sgm[:], bank[bk][:], ALU.mult,
                               after=[done, held["sig"], held.get("mval_used")])
                    held[f"bank{bk}"] = held["sig_used"] = t
                    if second:
                        t = dve.do(nc.vector.tensor_tensor, mval[:], mval[:], pk, ALU.add, after=[t])
                        held["mval_used"] = to_hi_lo(mval[:], m_hi[:, one, :].rearrange("p a n -> p (a n)"),
                                                     m_lo[:, one, :].rearrange("p a n -> p (a n)"), [t])
                tiles += [wtile(win2[:, ds(base_ + i * 2 * P + j * P, P)], a_in, 2 * j, gate_evac),
                          wtile(w[0][:, ds(i * 2 * P + j * P, P)], b_in, 2 * j + 1, w_evac)]
            return dense(tiles, nxt)
        return body

    ssm_branch = branch(GS2, w_branch_ssm_2, False)
    m.loop("ssm_branch", KD // 2, lambda i: run(ssm_branch(i, KD * P)))
    m.fence()
    tw = Memory(nc, aw_base, nc.sbuf_usable_end)
    F = lambda name, shape=(P, T): tw.take("t_" + name, list(shape))
    sa = [F(f"st{j}") for j in range(3)]
    qw, kw, vtok, szz = F("q"), F("k"), F("vtok"), F("sz")
    nfB, nfM = F("nfB", (P, 2, T)), F("nfM", (P, 2, T))
    Sx = [F(f"S{j}") for j in range(3)]
    PT = [F(f"PT{j}") for j in range(2)]
    on, yo = F("on", (P, NT, P)), F("yo")
    stat = F("stat", (P, 8, 8))

    def gate_tile(i):
        def evac(done):
            held["bank1"] = held["sz"] = act.do(nc.scalar.activation, szz[:], bank[1][:], ACT.Silu, after=[done])
        return [wtile(win2[:, ds(ZA2 + i * P, P)], a_in, 1, evac)]

    def qkv_tiles(i):
        def evac(j, bk, scale):
            def go(done):
                held[f"bank{bk}"] = held[f"st{j}"] = act.do(nc.scalar.activation, sa[j][:], bank[bk][:], ACT.Copy,
                                                            scale=scale, after=[done, held.get(f"used{j}")])
            return go
        return [wtile(win2[:, ds(b_ + i * P, P)], a_in, j % 2, evac(j, j % 2, 0.125 if j == 0 else 1.0))
                for j, b_ in enumerate((Q2, K2, V2))]

    def att_mix(i):
        held["sz"] = None
        before = m.all_now()
        for e in (act, dve, pool):
            e.wait(*before)
        rows_t = rows_in.mark(nc.scalar.dma_start(
            nfB[:], scratch[ds(i * 2 + NFROW, 2), :].partition_broadcast(P)), 16)
        tq = dve.do(nc.vector.tensor_copy, qw[:], sa[0][:], after=[held["st0"]])
        tk = dve.do(nc.vector.tensor_copy, kw[:], sa[1][:], after=[held["st1"]])
        held["used0"], held["used1"] = tq, tk
        yield 3
        pe.wait(*before)
        for t in range(NT):
            cc = slice(t * P, (t + 1) * P)
            ins = nc.tensor.transpose(bank[2][:, cc], sa[2][:, cc], ident[:])
        t = held["used2"] = pe.count.mark(ins)
        tvt = act.do(nc.scalar.activation, vtok[:], bank[2][:], ACT.Copy, after=[t])
        for a in range(2):
            tnf = dve.do(nc.vector.tensor_tensor, v3(nfM[:, a, :]), v3(nfB[:, a, :]), across(negmask[:]), ALU.add,
                         after=[rows_t])
        yield 2
        units = [(a, qb) for a in range(2) for qb in range(NT)]
        sread, exped, ptread = {}, {}, {}

        def scores(u):
            a, qb = units[u]
            n = (qb + 1) * P
            rows_ = slice(64 * a, 64 * a + 64)
            b_ = bank[3 + u % 2]
            S = Sx[u % 3]
            t = pe.do(nc.tensor.matmul, b_[:, 0:n], qw[rows_, qb * P:n], kw[rows_, 0:n], start=True, stop=True,
                      after=[tq, tk, sread.get(u - 2)])
            st = stat[:, u, :]
            dve.do(nc.vector.memset, st[:, 6:7] if qb else st[:, 1:2], NEG, after=[t, tnf, ptread.get(u - 3)])
            t = dve.do(nc.vector.tensor_tensor_reduce, S[:, qb * P:n], b_[:, qb * P:n], nfM[:, a, qb * P:n], 1.0, NEG,
                       ALU.add, ALU.max, st[:, 0:1])
            if qb:
                t = dve.do(nc.vector.tensor_tensor_reduce, S[:, 0:qb * P], b_[:, 0:qb * P], nfB[:, a, 0:qb * P], 1.0, NEG,
                           ALU.add, ALU.max, st[:, 1:2])
            sread[u] = t
            t = dve.do(nc.vector.tensor_scalar, st[:, 2:3], st[:, 0:1], st[:, 1:2], -1.0, ALU.max, ALU.mult, after=[t])
            t = act.do(nc.scalar.activation, S[:, 0:n], S[:, 0:n], ACT.Exp, bias=st[:, 2:3], accum_out=st[:, 3:4], after=[t])
            dve.do(nc.vector.reciprocal, st[:, 4:5], st[:, 3:4], after=[t])
            exped[u] = t

        scores(0)
        yield
        scores(1)
        yield
        copied = {}

        def values(u):
            a, qb = units[u]
            pe.wait(copied[u], tvt, held["pv"])
            for kb_ in range(qb + 1):
                ins = nc.tensor.matmul(bank[7][:, 0:64], PT[u % 2][:, kb_ * P:(kb_ + 1) * P],
                                       vtok[:, kb_ * P + a * 64:kb_ * P + a * 64 + 64], start=(kb_ == 0), stop=(kb_ == qb))
            t = pe.count.mark(ins)
            held["pv"] = dve.do(nc.vector.tensor_scalar, on[:, qb, a * 64:a * 64 + 64], bank[7][:, 0:64], stat[:, u, 4:5],
                                None, ALU.mult, after=[t])

        held["pv"] = None
        for u, (a, qb) in enumerate(units):
            if u + 2 < len(units):
                scores(u + 2)
                yield
            pb_ = bank[5 + u % 2]
            pe.wait(exped[u], copied.get(u - 2))
            for kb_ in range(qb + 1):
                ins = nc.tensor.transpose(pb_[:, kb_ * P:(kb_ + 1) * P], Sx[u % 3][:, kb_ * P:(kb_ + 1) * P], ident[:])
            t = ptread[u] = pe.count.mark(ins)
            n = (qb + 1) * P
            copied[u] = t = act.do(nc.scalar.activation, PT[u % 2][:, 0:n], pb_[:, 0:n], ACT.Copy, after=[t])
            yield
            if u:
                values(u - 1)
        yield 2
        values(len(units) - 1)
        yield 2
        pe.wait(held["pv"])
        for t in range(NT):
            ins = nc.tensor.transpose(bank[2][:, t * P:(t + 1) * P], on[:, t, :], ident[:])
        t = pe.count.mark(ins)
        t = dve.do(nc.vector.tensor_tensor, yo[:], szz[:], bank[2][:], ALU.mult, after=[t, queued("sz")])
        one = ds(i, 1)
        to_hi_lo(yo[:], b_hi[:, one, :].rearrange("p a n -> p (a n)"), b_lo[:, one, :].rearrange("p a n -> p (a n)"), [t])
        yield

    for j in range(3):
        held[f"used{j}"] = None
    run(dense(qkv_tiles(0), KD * P))
    m.loop("attention", HS // 2 - 1, lambda i: weave(att_mix(i), dense(gate_tile(i) + qkv_tiles(i + 1), KD * P), 1.15))
    weave(att_mix(HS // 2 - 1), dense(gate_tile(HS // 2 - 1), KD * P), 0.5)
    m.fence()
    held["sig_used"] = held["mval_used"] = None
    att_branch = branch(GA2, w_branch_att_2, True)
    m.loop("att_branch", KD // 2, lambda i: run(att_branch(i, KD * P)))
    m.fence()

    fin = nc.alloc_sbuf_tensor_at("fin", [P, KD, T], F32, offset=fin_at)

    def out_evac(mt, bk):
        def go(done):
            t = dve.do(nc.vector.tensor_copy, fin[:, mt, :], bank[bk][:], after=[done])
            held[f"bank{bk}"] = t
            held["sum"] = squares(mt, fin[:, mt, :], [sq2[0][:], sq2[1][:]], acc[:], [t])
        return go

    held["acc"] = held["sq0"] = held["sq1"] = None
    run(dense([wtile(w_out_2[0][:, mt * P:(mt + 1) * P], lambda k: (m_hi[:, k, :], m_lo[:, k, :]), mt % 2,
                     out_evac(mt, mt % 2)) for mt in range(KD)], 0))
    rt = inv_rms(acc[:], rstd, 2, D, [held["sum"]])
    for k in range(KD):
        t = dve.do(nc.vector.scalar_tensor_tensor, fin[:, k, :], fin[:, k, :], col_a[:, POST + k:POST + k + 1], rstd[:],
                   ALU.mult, ALU.mult, after=[rt])
        dve.do(nc.vector.tensor_tensor, fin[:, k, :], fin[:, k, :], xT[:, k, :], ALU.add, after=[t])
    store(fin)


_INS = ["x", "c", "w_ada", "b_ada", "norm1_w", "w_in", "conv_qkv_w", "A_log", "dt_bias", "gdn_norm_w",
        "conv_short_w", "w_out", "norm2_w", "w_gate", "w_up", "w_down", "norm_f_w", "pre_norm_g_2", "w_in_2",
        "conv_w_2", "conv_b_2", "dt_bias_2", "a_log_2", "d_skip_2", "ssm_norm_g_2", "fgate_b_2",
        "w_branch_ssm_2", "w_branch_att_2", "w_out_2", "post_norm_g_2"]
STOP = 0


def kernel(**inputs):
    import numpy as np
    import concourse.bacc as bacc
    from concourse.bass_utils import run_bass_kernel_spmd as run

    arrays = {f"in_{name}": np.ascontiguousarray(inputs[name]) for name in _INS}
    learned = {}
    for _ in range(2):
        nc = bacc.Bacc("TRN2", target_bir_lowering=False, num_devices=1)
        args = [nc.dram_tensor(n, a.shape, mybir.dt.from_np(a.dtype), kind="ExternalInput").ap()
                for n, a in arrays.items()]
        args.append(nc.dram_tensor("out", inputs["x"].shape, F32, kind="ExternalOutput").ap())
        program(nc, learned, STOP, *args)
    r = run(nc, [arrays], core_ids=[0])
    return r.results[0]["out"]
```
